# Optimizing a Trainium2 kernel written in Bass

```python
import jax, jax.numpy as jnp
from jax import lax
import numpy as np

D_MODEL = 1024
BATCH = 1
SEQ = 512
DEPTH = 1

CHUNK = 64
Q_BLOCK = 128
PLE_DIM = 256
CONV_DIM = D_MODEL // 2
CONV_WIDTH = 3
SB_HEADS = 8
SB_HEAD_DIM = 64
SB_DIM = SB_HEADS * SB_HEAD_DIM
MIX_WIDTH = CONV_DIM + SB_DIM
IN_PROJ_DIM = 3 * CONV_DIM + 3 * SB_DIM
D_FF = 2816
FFN_RES = 0.5
EPS = 1e-6

kernel_name = "hybrid_shortconv_stickbreaking_macaron_block"

def _rmsnorm(x, g):
    xf = x.astype(jnp.float32)
    y = xf * lax.rsqrt(jnp.mean(xf * xf, axis=-1, keepdims=True) + EPS)
    return (y * g.astype(jnp.float32)).astype(x.dtype)

def _swiglu(h, w_gate, w_up, w_down):
    return (jax.nn.silu(h @ w_gate) * (h @ w_up)) @ w_down

def _short_gated_conv(b, c, u, conv_w, conv_b):
    z = c * u
    rhs = conv_w[:, None, :].astype(z.dtype)
    y = lax.conv_general_dilated(
        z, rhs, window_strides=(1,), padding=[(CONV_WIDTH - 1, 0)],
        dimension_numbers=("NWC", "WIO", "NWC"), feature_group_count=CONV_DIM)
    return b * (y + conv_b.astype(z.dtype))

def _stick_breaking(q, k, v):
    S = q.shape[2]
    scale = SB_HEAD_DIM ** -0.5
    outs = []
    for t0 in range(0, S, Q_BLOCK):
        kl = t0 + Q_BLOCK
        qs = q[:, :, t0:t0 + Q_BLOCK]
        ks = k[:, :, :kl]
        vs = v[:, :, :kl]
        z = jnp.einsum("bhqd,bhkd->bhqk", qs, ks) * scale
        t_idx = t0 + jnp.arange(Q_BLOCK)[:, None]
        s_idx = jnp.arange(kl)[None, :]
        causal = s_idx < t_idx
        log_keep = jnp.where(causal, jax.nn.log_sigmoid(-z), 0.0)
        later = lax.cumsum(log_keep, axis=3, reverse=True) - log_keep
        a = jnp.where(causal, jnp.exp(jax.nn.log_sigmoid(z) + later), 0.0)
        outs.append(jnp.einsum("bhqk,bhkd->bhqd", a, vs))
    return jnp.concatenate(outs, axis=2)

def setup_inputs(seed: int = 0) -> dict:
    key = jax.random.key(seed)
    ks = jax.random.split(key, 24)
    f32 = jnp.float32

    def w(k, shape, fan_in):
        return jax.random.normal(k, shape, f32) * (fan_in ** -0.5)

    def gain(k, shape):
        return 1.0 + 0.05 * jax.random.normal(k, shape, f32)

    return {
        "x": jax.random.normal(ks[0], (BATCH, SEQ, D_MODEL), f32),
        "p": jax.random.normal(ks[1], (DEPTH, BATCH, SEQ, PLE_DIM), f32),
        "ffn1_norm": gain(ks[2], (DEPTH, D_MODEL)),
        "ffn1_w_gate": w(ks[3], (DEPTH, D_MODEL, D_FF), D_MODEL),
        "ffn1_w_up": w(ks[4], (DEPTH, D_MODEL, D_FF), D_MODEL),
        "ffn1_w_down": w(ks[5], (DEPTH, D_FF, D_MODEL), D_FF),
        "mix_norm": gain(ks[6], (DEPTH, D_MODEL)),
        "w_in": w(ks[7], (DEPTH, D_MODEL, IN_PROJ_DIM), D_MODEL),
        "conv_w": w(ks[8], (DEPTH, CONV_WIDTH, CONV_DIM), CONV_WIDTH),
        "conv_b": 0.02 * jax.random.normal(ks[9], (DEPTH, CONV_DIM), f32),
        "q_norm": gain(ks[10], (DEPTH, SB_HEAD_DIM)),
        "k_norm": gain(ks[11], (DEPTH, SB_HEAD_DIM)),
        "w_out": w(ks[12], (DEPTH, MIX_WIDTH, D_MODEL), MIX_WIDTH),
        "ffn2_norm": gain(ks[13], (DEPTH, D_MODEL)),
        "ffn2_w_gate": w(ks[14], (DEPTH, D_MODEL, D_FF), D_MODEL),
        "ffn2_w_up": w(ks[15], (DEPTH, D_MODEL, D_FF), D_MODEL),
        "ffn2_w_down": w(ks[16], (DEPTH, D_FF, D_MODEL), D_FF),
        "ple_norm": gain(ks[17], (DEPTH, D_MODEL)),
        "ple_w_gate": w(ks[18], (DEPTH, D_MODEL, D_MODEL), D_MODEL),
        "ple_w_proj": w(ks[19], (DEPTH, PLE_DIM, D_MODEL), PLE_DIM),
    }

def reference(x, p, ffn1_norm, ffn1_w_gate, ffn1_w_up, ffn1_w_down, mix_norm, w_in,
              conv_w, conv_b, q_norm, k_norm, w_out, ffn2_norm, ffn2_w_gate, ffn2_w_up,
              ffn2_w_down, ple_norm, ple_w_gate, ple_w_proj):
    B, S, _ = x.shape
    for i in range(DEPTH):
        x = x + FFN_RES * _swiglu(_rmsnorm(x, ffn1_norm[i]), ffn1_w_gate[i], ffn1_w_up[i], ffn1_w_down[i])

        h = _rmsnorm(x, mix_norm[i])
        proj = h @ w_in[i]
        b_g, c_g, u, q, k, v = jnp.split(
            proj, np.cumsum([CONV_DIM, CONV_DIM, CONV_DIM, SB_DIM, SB_DIM]).tolist(), axis=-1)

        y_conv = _short_gated_conv(b_g, c_g, u, conv_w[i], conv_b[i])

        def heads(t):
            return t.reshape(B, S, SB_HEADS, SB_HEAD_DIM).transpose(0, 2, 1, 3).astype(jnp.float32)
        qh = _rmsnorm(heads(q), q_norm[i])
        kh = _rmsnorm(heads(k), k_norm[i])
        y_sb = _stick_breaking(qh, kh, heads(v))
        y_sb = y_sb.transpose(0, 2, 1, 3).reshape(B, S, SB_DIM).astype(x.dtype)

        x = x + jnp.concatenate([y_conv, y_sb], axis=-1) @ w_out[i]

        x = x + FFN_RES * _swiglu(_rmsnorm(x, ffn2_norm[i]), ffn2_w_gate[i], ffn2_w_up[i], ffn2_w_down[i])

        gate = jax.nn.sigmoid(_rmsnorm(x, ple_norm[i]) @ ple_w_gate[i])
        x = x + gate * (p[i].astype(x.dtype) @ ple_w_proj[i])
    return x


_drawn_inputs = setup_inputs


def setup_inputs(seed=0):
    import zlib

    import numpy as np

    out = dict(_drawn_inputs(seed))
    spreads = {}
    factors = {'conv_b': 5.607, 'q_norm': 6.599, 'k_norm': 7.207, 'ffn2_norm': 3.683, 'ple_norm': 8.0}
    for name, (base, spread) in spreads.items():
        noise = np.random.default_rng([zlib.crc32(name.encode()), seed]).standard_normal(out[name].shape)
        drawn = base * np.exp(spread * noise) if base else spread * noise
        out[name] = __import__('jax').numpy.asarray(drawn.astype(out[name].dtype))
    for name, factor in factors.items():
        out[name] = (out[name] * factor).astype(out[name].dtype)
    return out
```

```python
from contextlib import ExitStack

import numpy as np

import concourse.bass as bass
from concourse import mybir

F32 = mybir.dt.float32
F32R = mybir.dt.float32r
BF16 = mybir.dt.bfloat16
ACT = mybir.ActivationFunctionType
ALU = mybir.AluOpType

P = 128
T = 512
D = 1024
KD = D // P
F = 2816
KF = F // P
KH = KF // 2
PK = 256 // P
CT = 4
HD = 64
QB = T // P
EPS = 1e-6
BLOCKED = -1e30

N_GU = 2 * KF
N_DN = 2 * KD
N_IN = 6 * CT
N_WO = 8
F1, D1 = 0, N_GU
MX = D1 + N_DN
WO = MX + N_IN
F2 = WO + N_WO
D2 = F2 + N_GU
PL = D2 + N_DN
UNITS = PL + KD
RAW = 4


def raw_plan():
    slot = [u % 2 if MX <= u < WO else u % RAW for u in range(UNITS)]
    fills, previous, last = [], [], {}
    for u, s in enumerate(slot):
        previous.append(last.get(s))
        last[s] = u
        fills.append(slot[:u + 1].count(s))
    return slot, fills, previous


SLOT, FILLS, PREVIOUS = raw_plan()


def along(table, u, stride, n):
    step = table[u + stride] - table[u] if n > 1 else 0
    assert all(table[u + i * stride] == table[u] + i * step for i in range(n))
    return table[u], step


def build(nc, xT, pT, params, gu1, dn1, w_in, w_out, gu2, dn2, ple, outT):
    ctx = ExitStack()
    with ctx:
        def sb(name, shape, dt=F32, stack=None):
            return (stack or ctx).enter_context(nc.sbuf_tensor(name, shape, dt))

        def sem(name):
            return ctx.enter_context(nc.semaphore(name))

        x = sb("x", [P, KD, T])
        xh = sb("xh", [P, KD, T], F32R)
        xl = sb("xl", [P, KD, T], F32R)
        raw = sb("raw", [P, RAW, KH * P])
        wh = sb("wh", [P, 2, KH * P], F32R)
        wl = sb("wl", [P, 2, KH * P], F32R)
        rms = sb("rms", [P, T])
        sqacc = sb("sqacc", [P, T])
        sq = sb("sq", [P, 2, T])
        var = sb("var", [P, T])
        y0 = sb("y0", [P, T])
        nw = sb("nw", [P, T])
        par = sb("par", [P, 50])
        one_col = sb("one_col", [P, 1])
        ones = sb("ones", [P, P])
        headones = sb("headones", [P, P])
        negtri = sb("negtri", [P, P])
        negones = sb("negones", [P, P])
        ident = sb("ident", [P, P])
        identb = sb("identb", [P, P], BF16)
        blocked = sb("blocked", [P, P], BF16)
        gq8 = sb("gq8", [P, 1])
        pad = sb("pad", [P, 4])
        act_in = sb("act_in", [P, 2, T])
        upr = sb("upr", [P, T])
        hid = sb("hid", [P, T])
        ffn_only = ExitStack()
        hh = sb("hh", [P, KF, T], F32R, ffn_only)
        hl = sb("hl", [P, KF, T], F32R, ffn_only)
        ffn_only.close()
        mix_only = ExitStack()
        qt = sb("qt", [P, T], F32, mix_only)
        kt = sb("kt", [P, T], F32, mix_only)
        vt = sb("vt", [P, T], F32, mix_only)
        qn = sb("qn", [P, T], F32, mix_only)
        kn = sb("kn", [P, T], F32, mix_only)
        vtok = sb("vtok", [P, QB, P], F32, mix_only)
        bt = sb("bt", [P, T], F32, mix_only)
        cgate = sb("cgate", [P, T], F32, mix_only)
        ut = sb("ut", [P, T], F32, mix_only)
        cz = sb("cz", [P, T], F32, mix_only)
        cy = sb("cy", [P, T], F32, mix_only)
        vq = sb("vq", [P, T], F32, mix_only)
        yq = sb("yq", [P, T], F32, mix_only)
        nq = sb("nq", [P, T], F32, mix_only)
        sqq = sb("sqq", [P, T], F32, mix_only)
        att = [sb(f"att{j}", [P, 2, T - P * j], F32, mix_only) for j in range(QB)]
        sp_ = [sb(f"sp{j}", [P, 2, T - P * j], F32, mix_only) for j in range(QB)]
        ych = sb("ych", [P, CT, T], F32R, mix_only)
        ycl = sb("ycl", [P, CT, T], F32R, mix_only)
        ysh = sb("ysh", [P, CT, T], F32R, mix_only)
        ysl = sb("ysl", [P, CT, T], F32R, mix_only)
        mix_only.close()
        ple_only = ExitStack()
        praw = sb("praw", [P, PK, T], F32, ple_only)
        ph = sb("ph", [P, PK, T], F32R, ple_only)
        pl = sb("pl", [P, PK, T], F32R, ple_only)
        ple_only.close()

        ps = ctx.enter_context(nc.psum_tensor("ps", [P, 8, T], F32))
        ZA, ZB, BO, BN = 2, 4, 6, 7

        raw_in = [sem(f"raw_in{s}") for s in range(RAW)]
        hi_done, lo_done, unit_done = sem("hi_done"), sem("lo_done"), sem("unit_done")
        x_in = [sem(f"x_in{c}") for c in range(KD // 2)]
        par_in, p_in, gq_ok = sem("par_in"), sem("p_in"), sem("gq_ok")
        const_step = sem("const_step")
        x_new, xh_done, xl_done = sem("x_new"), sem("xh_done"), sem("xl_done")
        sq_done, acc_done = sem("sq_done"), sem("acc_done")
        sum_done, var_done, guess_done = sem("sum_done"), sem("var_done"), sem("guess_done")
        newton, rms_done, ln_done = sem("newton"), sem("rms_done"), sem("ln_done")
        out_ready, stored = sem("out_ready"), sem("stored")

        g_col = lambda n, k: par[:, 8 * n + k:8 * n + k + 1]
        conv_w = lambda t, tap: par[:, 32 + 3 * t + tap:33 + 3 * t + tap]
        conv_b = lambda t: par[:, 44 + t:45 + t]
        gq, gk = par[:, 48:49], par[:, 49:50]

        block = ctx.enter_context(nc.Block())

        FFN = []
        for n, (u0, d0) in enumerate(((F1, D1), (F2, D2))):
            FFN.append(dict(
                n=n, u0=u0, d0=d0,
                banks=sem(f"ffn{n}_banks"), silu=sem(f"ffn{n}_silu"), hid=sem(f"ffn{n}_hid"),
                hh=sem(f"ffn{n}_hh"), hl=sem(f"ffn{n}_hl")))
        m_evac = sem("mix_evac")
        q_sq, k_sq = sem("q_sq"), sem("k_sq")
        hsum, hvar, hln, hguess, hnewton = (sem(s) for s in ("hsum", "hvar", "hln", "hguess", "hnewton"))
        qk_ready = sem("qk_ready")
        v_turned, v_ready = sem("v_turned"), sem("v_ready")
        z_ready, nabs, e_done, l_done, sp_done = (sem(s) for s in ("z_ready", "nabs", "e_done", "l_done", "sp_done"))
        later_done, a_done = sem("later_done"), sem("a_done")
        o_done, o_hi, o_free = sem("o_done"), sem("o_hi"), sem("o_free")
        conv = sem("conv_step")
        yc_done = sem("yc_done")
        wo_evac, wo_even = sem("wo_evac"), sem("wo_even")
        ple_t, ple_s, ple_m, p_hi, p_lo = (sem(s) for s in ("ple_t", "ple_s", "ple_m", "p_hi", "p_lo"))

        NORM1, NORMX, NORM2, NORMP = range(4)
        xl_before = [8 * n for n in range(5)]
        X_AT = [None, 2, 2 + KD, 2 + 2 * KD]
        X_LAST = 2 + 3 * KD

        @block.sync
        def _(sp):
            def load(src, u, nk, i=0, stride=0, n=1):
                if PREVIOUS[u] is not None:
                    a, b = along(PREVIOUS, u, stride, n)
                    sp.wait_ge(lo_done, a + 1 + i * b)
                sp.dma_start(raw[:, SLOT[u], 0:nk * P], src).then_inc(raw_in[SLOT[u]], 16)

            sp.dma_start(par[:, :], params[:, :]).then_inc(par_in, 16)
            for c in range(KD // 2):
                sp.dma_start(x[:, 2 * c:2 * c + 2, :], xT[:, 2 * c:2 * c + 2, :]).then_inc(x_in[c], 16)
                if c < 2:
                    load(gu1[c], F1 + c, KD)

            def ffn_loads(ff, gu, dn, done):
                for u in range(done, RAW):
                    load(gu[u], ff["u0"] + u, KD)
                n = N_GU // RAW - 1
                with sp.Fori(0, n) as i:
                    for j in range(RAW):
                        load(gu[bass.ds(i * RAW + RAW + j, 1)].rearrange("a p n -> (a p) n"),
                             ff["u0"] + RAW + j, KD, i, RAW, n)
                n = N_DN // RAW
                with sp.Fori(0, n) as i:
                    for j in range(RAW):
                        load(dn[bass.ds(i * RAW + j, 1)].rearrange("a p n -> (a p) n"),
                             ff["d0"] + j, KH, i, RAW, n)

            ffn_loads(FFN[0], gu1, dn1, 2)
            for u in range(3):
                load(w_in[u], MX + u, KD)
            with sp.Fori(0, CT - 1) as i:
                for j in range(6):
                    load(w_in[bass.ds(i * 6 + 3 + j, 1)].rearrange("a p n -> (a p) n"),
                         MX + 3 + j, KD, i, 6, CT - 1)
            for u in range(N_IN - 3, N_IN):
                load(w_in[u], MX + u, KD)
            for u in range(N_WO):
                load(w_out[u], WO + u, KD)
            ffn_loads(FFN[1], gu2, dn2, 0)
            for u in range(2):
                load(ple[u], PL + u, KD + PK)
            sp.wait_ge(unit_done, PL)
            sp.dma_start(praw[:, :, :], pT[:, :, :]).then_inc(p_in, 16)
            for u in range(2, KD):
                load(ple[u], PL + u, KD + PK)
            for m in range(KD):
                sp.wait_ge(out_ready, m + 1)
                sp.dma_start(outT[:, m, :], x[:, m, :]).then_inc(stored, 16)
            sp.wait_ge(stored, 16 * KD)

        @block.gpsimd
        def _(pool):
            def select(t, op, base, pattern, mult, fill, step):
                pool.wait_ge(const_step, step)
                pool.affine_select(out=t, in_=t, compare_op=op, fill=fill, base=base, pattern=pattern,
                                   channel_multiplier=mult).then_inc(const_step, 1)

            pool.memset(one_col[:, :], 1.0).then_inc(const_step, 1)
            pool.memset(ones[:, :], 1.0).then_inc(const_step, 1)
            pool.memset(sqacc[:, :], 0.0).then_inc(acc_done, 1)

            def lo(u, nk, i=0, stride=0):
                pool.wait_ge(hi_done, u + 1 + i * stride)
                pool.tensor_tensor(wl[:, u % 2, 0:nk * P], raw[:, SLOT[u], 0:nk * P],
                                   wh[:, u % 2, 0:nk * P].bitcast(F32), ALU.subtract).then_inc(lo_done, 1)

            def add_square(norm, m, b, i=0, step=0):
                pool.wait_ge(sq_done, 8 * norm + m + 1 + i * step)
                pool.wait_ge(acc_done, 9 * norm + m + 1 + i * step)
                pool.tensor_tensor(sqacc[:, :], sqacc[:, :], sq[:, b, :], ALU.add).then_inc(acc_done, 1)

            lo(F1, KD)
            for k in range(KD):
                add_square(0, k, k % 2)
                if k == 1:
                    lo(F1 + 1, KD)
            fills = [(headones, 1.0), (negtri, -1.0), (negones, -1.0), (ident, 0.0), (identb, 0.0), (blocked, 0.0)]
            for t, v in fills:
                pool.memset(t[:, :], v).then_inc(const_step, 1)
            n = 2 + len(fills)
            select(headones[:, 0:HD], ALU.is_ge, HD - 1, [[0, HD]], -1, 0.0, n)
            select(headones[:, HD:P], ALU.is_ge, -HD, [[0, HD]], 1, 0.0, n)
            select(negtri[:, :], ALU.is_ge, 0, [[-1, P]], 1, 0.0, n)
            select(ident[:, :], ALU.not_equal, 0, [[-1, P]], 1, 1.0, n)
            select(identb[:, :], ALU.not_equal, 0, [[-1, P]], 1, 1.0, n)
            select(blocked[:, :], ALU.is_gt, 0, [[1, P]], -1, BLOCKED, n)

            def new_sum(norm):
                pool.wait_ge(sum_done, norm)
                pool.memset(sqacc[:, :], 0.0).then_inc(acc_done, 1)

            def ffn(ff, first, nxt, nxt_nk, norm):
                u0, d0 = ff["u0"], ff["d0"]
                for u in range(first, 2):
                    lo(u0 + u, KD)
                n = N_GU // RAW - 1
                with pool.Fori(0, n) as i:
                    for j in range(RAW):
                        lo(u0 + 2 + j, KD, i, RAW)
                lo(u0 + N_GU - 2, KD)
                lo(u0 + N_GU - 1, KD)
                new_sum(norm)
                lo(d0, KH)
                lo(d0 + 1, KH)
                with pool.Fori(0, KD // 2 - 1) as i:
                    for j in range(2):
                        lo(d0 + 2 + 2 * j, KH, i, 4)
                        lo(d0 + 3 + 2 * j, KH, i, 4)
                        add_square(norm, j, j, i, 2)
                for m in range(KD - 2, KD):
                    for e in range(2):
                        u = d0 + 2 * m + 2 + e
                        if u < d0 + N_DN:
                            lo(u, KH)
                        else:
                            lo(nxt + u - d0 - N_DN, nxt_nk)
                    add_square(norm, m, m % 2)

            ffn(FFN[0], 2, MX, KD, 1)
            lo(MX + 2, KD)
            with pool.Fori(0, CT - 1) as i:
                for j in range(6):
                    lo(MX + 3 + j, KD, i, 6)
            for u in range(MX + N_IN - 3, WO + 4):
                lo(u, KD)
            new_sum(2)
            lo(WO + 4, KD)
            lo(WO + 5, KD)
            for n in range(4):
                u = WO + 6 + n
                lo(u, KD)
                for e in range(2):
                    add_square(2, 2 * n + e, e)
            ffn(FFN[1], 2, PL, KD + PK, 3)
            for u in range(PL + 2, UNITS):
                lo(u, KD + PK)

        @block.scalar
        def _(act):
            def hi(u, nk, i=0, stride=0, n=1):
                a, b = along(FILLS, u, stride, n)
                act.wait_ge(raw_in[SLOT[u]], 16 * a + i * (16 * b))
                if u >= 2:
                    act.wait_ge(unit_done, u - 1 + i * stride)
                act.activation(wh[:, u % 2, 0:nk * P], raw[:, SLOT[u], 0:nk * P], ACT.Copy).then_inc(hi_done, 1)

            def guess(norm):
                act.preload_act_table_set("natural_log_exp_and_others")
                act.wait_ge(var_done, norm + 1)
                act.activation(y0[:, :], var[:, :], ACT.Ln).then_inc(ln_done, 1)
                act.wait_ge(ln_done, norm + 1)
                act.activation(y0[:, :], y0[:, :], ACT.Exp, scale=-0.5).then_inc(guess_done, 1)

            hi(F1, KD)
            act.wait_ge(par_in, 16)
            for k in range(KD):
                act.wait_ge(x_in[k // 2], 16)
                if k >= 2:
                    act.wait_ge(acc_done, k)
                act.activation(sq[:, k % 2, :], x[:, k, :], ACT.Square).then_inc(sq_done, 1)
                if k == 0:
                    hi(F1 + 1, KD)

            def new_x(norm, m, b, i=0, step=0):
                act.wait_ge(x_new, X_AT[norm] + m + 1 + i * step)
                act.wait_ge(acc_done, 9 * norm + m + i * step)
                if step:
                    act.nop(nofuse=True)
                    xm = x[:, bass.ds(i * step + m, 1), :]
                    dst = xh[:, bass.ds(i * step + m, 1), :]
                    gain = par[:, bass.ds(i * step + m + 8 * norm, 1)]
                else:
                    xm, dst, gain = x[:, m, :], xh[:, m, :], g_col(norm, m)
                act.activation(dst, xm, ACT.Identity, scale=gain).then_inc(xh_done, 1)
                act.activation(sq[:, b, :], xm, ACT.Square).then_inc(sq_done, 1)

            def ffn(ff, nxt, nxt_nk, norm):
                u0, d0 = ff["u0"], ff["d0"]

                def silu(f, b, i=0, step=0):
                    act.wait_ge(ff["banks"], 4 + 2 * f + 1 + i * 2 * step)
                    act.activation(act_in[:, b, :], act_in[:, b, :], ACT.Silu).then_inc(ff["silu"], 1)

                hi(u0 + 2, KD)
                guess(norm - 1)
                silu(0, 0)
                hi(u0 + 3, KD)
                hi(u0 + 4, KD)
                silu(1, 1)
                hi(u0 + 5, KD)
                n = N_GU // RAW - 2
                with act.Fori(0, n) as i:
                    hi(u0 + 6, KD, i, 4, n)
                    silu(2, 0, i, 2)
                    hi(u0 + 7, KD, i, 4, n)
                    hi(u0 + 8, KD, i, 4, n)
                    silu(3, 1, i, 2)
                    hi(u0 + 9, KD, i, 4, n)
                hi(u0 + N_GU - 2, KD)
                silu(KF - 2, 0)
                hi(u0 + N_GU - 1, KD)
                hi(d0, KH)
                silu(KF - 1, 1)
                hi(d0 + 1, KH)
                n = KD // 2 - 1
                with act.Fori(0, n) as i:
                    for j in range(2):
                        hi(d0 + 2 + 2 * j, KH, i, 4, n)
                        hi(d0 + 3 + 2 * j, KH, i, 4, n)
                        new_x(norm, j, j, i, 2)
                for m in range(KD - 2, KD):
                    for e in range(2):
                        u = d0 + 2 * m + 2 + e
                        if u < d0 + N_DN:
                            hi(u, KH)
                        else:
                            hi(nxt + u - d0 - N_DN, nxt_nk)
                    new_x(norm, m, m % 2)

            ffn(FFN[0], MX, KD, 1)

            def head_guess(c, i=0):
                act.wait_ge(hvar, c + 1 + i)
                act.activation(yq[:, :], vq[:, :], ACT.Ln).then_inc(hln, 1)
                act.wait_ge(hln, c + 1 + i)
                act.activation(yq[:, :], yq[:, :], ACT.Exp, scale=-0.5).then_inc(hguess, 1)

            def softplus(j, n, z, i=0):
                act.wait_ge(z_ready, n + 1 + i)
                act.activation(att[j][:, :, :], ps[:, z:z + 2, 0:T - P * j], ACT.Abs).then_inc(nabs, 1)
                act.wait_ge(nabs, n + 1 + i)
                act.activation(att[j][:, :, :], att[j][:, :, :], ACT.Exp, scale=-1.0).then_inc(e_done, 1)
                act.wait_ge(e_done, n + 1 + i)
                act.activation(att[j][:, :, :], att[j][:, :, :], ACT.Ln, bias=one_col[:, :]).then_inc(l_done, 1)

            def weights(j, n, z, i=0):
                act.wait_ge(later_done, n + 1 + i)
                act.wait_ge(sp_done, n + 1 + i)
                w = T - P * j
                act.activation(att[j][:, :, :], ps[:, z:z + 2, 0:w], ACT.Exp).then_inc(a_done, 1)

            def head_square(t, evac, done, i=0, count=0):
                act.wait_ge(m_evac, evac + i * 6)
                if count is not None:
                    act.wait_ge(hsum, count + i * 2)
                act.activation(sqq[:, :], t[:, :], ACT.Square).then_inc(done, 1)

            def v_copy(c, i=0):
                act.wait_ge(v_turned, c + 1 + i)
                act.activation(vtok[:, :, :], ps[:, BN, :].rearrange("p (b d) -> p b d", b=QB), ACT.Copy).then_inc(v_ready, 1)

            def out_hi(c, i=None):
                act.wait_ge(o_done, (c if i is None else i) + 1)
                if i is None:
                    dst, src = ysh[:, c, :], ps[:, BO, :]
                else:
                    act.nop(nofuse=True)
                    dst, src = ysh[:, bass.ds(i, 1), :], ps[:, BO:BO + 1, :]
                act.activation(dst, src, ACT.Copy).then_inc(o_hi, 1)

            hi(MX + 2, KD)
            guess(1)
            head_square(qt, 1, q_sq, count=None)
            hi(MX + 3, KD)
            head_guess(0)
            head_square(kt, 2, k_sq, count=1)
            hi(MX + 4, KD)

            def pair(i, last):
                i4, i2, i6 = i * 4, i * 2, i * 6
                c = 0 if not last else CT - 1
                if last:
                    i4 = i2 = i6 = 0
                one = i if not last else 0
                b4, b2, b6 = 4 * c, 2 * c, 6 * c
                B = MX + 3 + b6
                n = CT - 1

                def hi6(local):
                    if last:
                        hi(B + local, KD)
                    else:
                        hi(B + local, KD, i, 6, n)
                head_guess(b2 + 1, i2)
                hi6(2)
                v_copy(c, one)
                softplus(3, b4, ZA, i4)
                softplus(2, b4 + 1, ZB, i4)
                hi6(3)
                hi6(4)
                weights(3, b4, ZA, i4)
                weights(2, b4 + 1, ZB, i4)
                softplus(1, b4 + 2, ZA, i4)
                hi6(5)
                if not last:
                    head_square(qt, 7, q_sq, i, 2)
                softplus(0, b4 + 3, ZB, i4)
                if not last:
                    head_guess(2, i2)
                    head_square(kt, 8, k_sq, i, 3)
                hi6(6)
                if last:
                    hi6(7)
                weights(1, b4 + 2, ZA, i4)
                weights(0, b4 + 3, ZB, i4)
                if not last:
                    hi6(7)
                    out_hi(0, i)
                else:
                    out_hi(CT - 1)

            with act.Fori(0, CT - 1) as i:
                pair(i, False)
            pair(0, True)
            hi(WO + 5, KD)
            for n in range(4):
                u = WO + 6 + n
                hi(u, KD)
                new_x(2, 2 * n, 0)
                new_x(2, 2 * n + 1, 1)
            ffn(FFN[1], PL, KD + PK, 3)

            for k in range(PK):
                act.wait_ge(p_in, 16)
                act.activation(ph[:, k, :], praw[:, k, :], ACT.Copy).then_inc(p_hi, 1)
            hi(PL + 2, KD + PK)
            guess(3)
            for m in range(KD):
                if 3 <= m + 2 < KD:
                    hi(PL + m + 2, KD + PK)
                act.wait_ge(ple_t, m + 1)
                act.activation(act_in[:, m % 2, :], act_in[:, m % 2, :], ACT.Sigmoid).then_inc(ple_s, 1)

        @block.vector
        def _(dve):
            def sharpen(count, v, y, t, dst, name, done, i=0):
                dve.scalar_tensor_tensor(t[:, :], y[:, :], -0.5, y[:, :], ALU.mult, ALU.mult).then_inc(name, 1)
                dve.wait_ge(name, 2 * count + 1 + i * 2)
                dve.tensor_tensor(t[:, :], t[:, :], v[:, :], ALU.mult).then_inc(name, 1)
                dve.wait_ge(name, 2 * count + 2 + i * 2)
                dve.scalar_tensor_tensor(dst[:, :], t[:, :], 1.5, y[:, :], ALU.add, ALU.mult).then_inc(done, 1)

            def rms_factor(norm):
                dve.wait_ge(sum_done, norm + 1)
                dve.tensor_scalar(var[:, :], ps[:, BN, :], 1.0 / D, EPS, ALU.mult, ALU.add).then_inc(var_done, 1)
                dve.wait_ge(guess_done, norm + 1)
                sharpen(norm, var, y0, nw, rms, newton, rms_done)
                dve.wait_ge(rms_done, norm + 1)

            dve.memset(pad[:, 0:1], 0.0).then_inc(x_new, 2)
            dve.memset(pad[:, 1:2], 0.0).then_inc(FFN[0]["banks"], 4)
            dve.memset(pad[:, 2:3], 0.0).then_inc(FFN[1]["banks"], 4)
            dve.memset(pad[:, 3:4], 0.0).then_inc(o_free, 1)
            dve.wait_ge(par_in, 16)
            dve.tensor_scalar(gq8[:, :], gq, HD ** -0.5, None, ALU.mult).then_inc(gq_ok, 1)
            for k in range(KD):
                dve.wait_ge(x_in[k // 2], 16)
                dve.tensor_scalar(xh[:, k, :], x[:, k, :], g_col(NORM1, k), None, ALU.mult).then_inc(xh_done, 1)
                dve.wait_ge(xh_done, k + 1)
                dve.scalar_tensor_tensor(xl[:, k, :], x[:, k, :], g_col(NORM1, k), xh[:, k, :].bitcast(F32),
                                         ALU.mult, ALU.subtract).then_inc(xl_done, 1)

            def new_x(norm, m, bank, scale, i=0, step=0):
                if step:
                    at = bass.ds(i * step + m, 1)
                    xm, h, l = x[:, at, :], xh[:, at, :], xl[:, at, :]
                    gain = par[:, bass.ds(i * step + m + 8 * norm, 1)]
                    src = ps[:, bank:bank + 1, :]
                else:
                    xm, h, l, gain, src = x[:, m, :], xh[:, m, :], xl[:, m, :], g_col(norm, m), ps[:, bank, :]
                dve.scalar_tensor_tensor(xm, src, scale, xm, ALU.mult, ALU.add).then_inc(x_new, 1)
                dve.wait_ge(xh_done, 8 * norm + m + 1 + i * step)
                dve.scalar_tensor_tensor(l, xm, gain, h.bitcast(F32), ALU.mult, ALU.subtract).then_inc(xl_done, 1)

            def ffn(ff, norm):
                u0, d0 = ff["u0"], ff["d0"]
                rms_factor(norm - 1)
                n = KF // 2
                with dve.Fori(0, n) as i:
                    for b in range(2):
                        dve.wait_ge(unit_done, u0 + 2 * b + 1 + i * 4)
                        dve.tensor_tensor(act_in[:, b, :], ps[:, 2 * b, :], rms[:, :], ALU.mult).then_inc(ff["banks"], 1)
                        dve.wait_ge(unit_done, u0 + 2 * b + 2 + i * 4)
                        dve.tensor_tensor(upr[:, :], ps[:, 2 * b + 1, :], rms[:, :], ALU.mult).then_inc(ff["banks"], 1)
                        dve.wait_ge(ff["banks"], 4 + 2 * b + 2 + i * 4)
                        dve.wait_ge(ff["silu"], b + 1 + i * 2)
                        dve.tensor_tensor(hid[:, :], act_in[:, b, :], upr[:, :], ALU.mult).then_inc(ff["hid"], 1)
                        dve.wait_ge(ff["hid"], b + 1 + i * 2)
                        at = bass.ds(i * 2 + b, 1)
                        dve.tensor_scalar(hh[:, at, :], hid[:, :], 1.0, None, ALU.mult).then_inc(ff["hh"], 1)
                        dve.wait_ge(ff["hh"], b + 1 + i * 2)
                        dve.tensor_tensor(hl[:, at, :], hid[:, :], hh[:, at, :].bitcast(F32), ALU.subtract).then_inc(ff["hl"], 1)
                with dve.Fori(0, KD // 2) as i:
                    for j in range(2):
                        dve.wait_ge(unit_done, d0 + 2 * j + 2 + i * 4)
                        new_x(norm, j, j, 0.5, i, 2)

            ffn(FFN[0], 1)

            def evac(dst, unit, bank, i=0):
                dve.wait_ge(unit_done, unit + 1 + i * 6)
                dve.tensor_tensor(dst[:, :], ps[:, bank, :], rms[:, :], ALU.mult).then_inc(m_evac, 1)

            def head_norm(c, t, gain, dst, i=0):
                dve.wait_ge(hsum, c + 1 + i)
                dve.tensor_scalar(vq[:, :], ps[:, BN, :], 1.0 / HD, EPS, ALU.mult, ALU.add).then_inc(hvar, 1)
                dve.wait_ge(hguess, c + 1 + i)
                dve.scalar_tensor_tensor(nq[:, :], yq[:, :], -0.5, yq[:, :], ALU.mult, ALU.mult).then_inc(hnewton, 1)
                dve.wait_ge(hnewton, 3 * c + 1 + i * 3)
                dve.tensor_tensor(nq[:, :], nq[:, :], vq[:, :], ALU.mult).then_inc(hnewton, 1)
                dve.wait_ge(hnewton, 3 * c + 2 + i * 3)
                dve.scalar_tensor_tensor(nq[:, :], nq[:, :], 1.5, yq[:, :], ALU.add, ALU.mult).then_inc(hnewton, 1)
                dve.wait_ge(hnewton, 3 * c + 3 + i * 3)
                dve.scalar_tensor_tensor(dst[:, :], t[:, :], gain, nq[:, :], ALU.mult, ALU.mult).then_inc(qk_ready, 1)

            def softplus(j, n, z, i=0):
                dve.wait_ge(l_done, n + 1 + i)
                w = T - P * j
                dve.scalar_tensor_tensor(sp_[j][:, :, :], ps[:, z:z + 2, 0:w], 0.0, att[j][:, :, :],
                                         ALU.max, ALU.add).then_inc(sp_done, 1)

            rms_factor(1)
            evac(qt, MX, 0)
            evac(kt, MX + 1, 1)
            dve.wait_ge(gq_ok, 1)
            head_norm(0, qt, gq8[:, :], qn)
            evac(vt, MX + 2, 0)

            def pair(i, last):
                c = CT - 1 if last else 0
                one = 0 if last else i
                i2, i4, i6 = one * 2, one * 4, one
                B = MX + 3 + 6 * c
                n_conv = 5 * c
                i5 = one * 5

                def bank(local):
                    return (3 + local) % 2

                def ev(dst, local):
                    evac(dst, B + local, bank(local), one)
                head_norm(2 * c + 1, kt, gk, kn, i2)
                ev(bt, 0)
                ev(cgate, 1)
                softplus(3, 4 * c, ZA, i4)
                softplus(2, 4 * c + 1, ZB, i4)
                ev(ut, 2)
                dve.wait_ge(m_evac, 6 * c + 6 + (0 if last else i * 6))
                dve.tensor_tensor(cz[:, :], cgate[:, :], ut[:, :], ALU.mult).then_inc(conv, 1)
                dve.wait_ge(conv, n_conv + 1 + i5)
                if last:
                    w = [conv_w(c, tap) for tap in range(3)]
                    bias = conv_b(c)
                    yh, yl = ych[:, c, :], ycl[:, c, :]
                else:
                    w = [par[:, bass.ds(i * 3 + (32 + tap), 1)] for tap in range(3)]
                    bias = par[:, bass.ds(i + 44, 1)]
                    yh, yl = ych[:, bass.ds(i, 1), :], ycl[:, bass.ds(i, 1), :]
                dve.tensor_scalar(cy[:, :], cz[:, :], w[2], bias, ALU.mult, ALU.add).then_inc(conv, 1)
                dve.wait_ge(conv, n_conv + 2 + i5)
                dve.scalar_tensor_tensor(cy[:, 1:T], cz[:, 0:T - 1], w[1], cy[:, 1:T], ALU.mult, ALU.add).then_inc(conv, 1)
                dve.wait_ge(conv, n_conv + 3 + i5)
                dve.scalar_tensor_tensor(cy[:, 2:T], cz[:, 0:T - 2], w[0], cy[:, 2:T], ALU.mult, ALU.add).then_inc(conv, 1)
                dve.wait_ge(conv, n_conv + 4 + i5)
                dve.tensor_tensor(cy[:, :], cy[:, :], bt[:, :], ALU.mult).then_inc(conv, 1)
                dve.wait_ge(conv, n_conv + 5 + i5)
                dve.tensor_scalar(yh, cy[:, :], 1.0, None, ALU.mult).then_inc(yc_done, 1)
                dve.wait_ge(yc_done, 2 * c + 1 + i2)
                dve.tensor_tensor(yl, cy[:, :], yh.bitcast(F32), ALU.subtract).then_inc(yc_done, 1)
                if last:
                    add_out(0, 0)
                    add_out(1, 1)
                if last:
                    add_out(2, 0)
                else:
                    ev(qt, 3)
                softplus(1, 4 * c + 2, ZA, i4)
                if last:
                    add_out(3, 1)
                softplus(0, 4 * c + 3, ZB, i4)
                if not last:
                    head_norm(2, qt, gq8[:, :], qn, i2)
                    ev(kt, 4)
                    dve.wait_ge(v_turned, 1 + i)
                    ev(vt, 5)
                    at = bass.ds(i, 1)
                    dve.wait_ge(o_hi, i + 1)
                    dve.tensor_tensor(ysl[:, at, :], ps[:, BO:BO + 1, :], ysh[:, at, :].bitcast(F32),
                                      ALU.subtract).then_inc(o_free, 1)
                else:
                    for m in range(4, KD - 1):
                        add_out(m, m % 2)
                    dve.wait_ge(o_hi, CT)
                    dve.tensor_tensor(ysl[:, CT - 1, :], ps[:, BO, :], ysh[:, CT - 1, :].bitcast(F32),
                                      ALU.subtract).then_inc(o_free, 1)
                    add_out(KD - 1, 1)

            def wo_tile_done(half):
                if half % 2:
                    dve.wait_ge(unit_done, WO + half // 2 + 1)
                else:
                    dve.wait_ge(wo_even, half // 2 + 1)

            def add_out(m, bank):
                wo_tile_done(m)
                dve.tensor_tensor(x[:, m, :], ps[:, bank, :], x[:, m, :], ALU.add).then_inc(wo_evac, 1)

            with dve.Fori(0, CT - 1) as i:
                pair(i, False)
            pair(0, True)
            dve.wait_ge(wo_evac, KD)
            for m in range(KD):
                wo_tile_done(KD + m)
                new_x(2, m, m % 2, 1.0)
            ffn(FFN[1], 3)

            for k in range(PK):
                dve.wait_ge(p_hi, k + 1)
                dve.tensor_tensor(pl[:, k, :], praw[:, k, :], ph[:, k, :].bitcast(F32), ALU.subtract).then_inc(p_lo, 1)
            rms_factor(3)
            for m in range(KD):
                b = m % 2
                dve.wait_ge(unit_done, PL + m + 1)
                dve.tensor_tensor(act_in[:, b, :], ps[:, 2 * b, :], rms[:, :], ALU.mult).then_inc(ple_t, 1)
                dve.wait_ge(ple_s, m + 1)
                dve.tensor_tensor(upr[:, :], ps[:, 2 * b + 1, :], act_in[:, b, :], ALU.mult).then_inc(ple_m, 1)
                dve.wait_ge(ple_m, m + 1)
                dve.tensor_tensor(x[:, m, :], x[:, m, :], upr[:, :], ALU.add).then_inc(out_ready, 1)

        @block.tensor
        def _(pe):
            def products(u, bank, ks, at, mh, ml, ready=None, first=True, last=True, i=0, stride=0, inc=unit_done):
                b = u % 2
                pe.wait_ge(lo_done, u + 1 + i * stride)
                for n, (k, a) in enumerate(zip(ks, at)):
                    if ready is not None:
                        pe.wait_ge(ready[0], ready[1] + k + 1)
                    w_hi, w_lo = wh[:, b, a * P:(a + 1) * P], wl[:, b, a * P:(a + 1) * P]
                    pe.matmul(ps[:, bank, :], w_hi, mh[:, k, :], start=first and n == 0, stop=False)
                    pe.matmul(ps[:, bank, :], w_hi, ml[:, k, :], start=False, stop=False)
                    mm = pe.matmul(ps[:, bank, :], w_lo, mh[:, k, :], start=False, stop=last and n == len(ks) - 1)
                if inc is not None:
                    mm.then_inc(inc, 1)

            def sum_squares(norm):
                if norm:
                    pe.wait_ge(var_done, norm)
                pe.wait_ge(acc_done, 9 * (norm + 1))
                pe.matmul(ps[:, BN, :], ones[:, :], sqacc[:, :], start=True, stop=True).then_inc(sum_done, 1)

            K8 = range(KD)

            def ffn(ff, norm):
                u0, d0 = ff["u0"], ff["d0"]
                ready = (xl_done, xl_before[norm])

                def four(i, base, peeled):
                    for j in range(4):
                        pe.wait_ge(ff["banks"], base + j + 1 + i * 4)
                        if peeled and norm and j < 2:
                            pe.wait_ge(x_new, X_AT[norm + 1] - 1 + j)
                        products(u0 + base + j, j, K8, K8, xh, xl, ready if j == 0 and peeled else None, i=i, stride=4)
                        if peeled and j == 0:
                            sum_squares(norm)
                four(0, 0, True)
                with pe.Fori(0, N_GU // 4 - 1) as i:
                    four(i, 4, False)
                pe.wait_ge(ff["banks"], 4 + N_GU - 2)
                with pe.Fori(0, KD // 2) as i:
                    for j in range(2):
                        pe.wait_ge(x_new, X_AT[norm + 1] - 1 + j + i * 2)
                        for e in range(2):
                            pe.wait_ge(ff["hl"], KH * (e + 1))
                            products(d0 + 2 * j + e, j, range(e * KH, (e + 1) * KH), range(KH), hh, hl,
                                     first=e == 0, last=e == 1, i=i, stride=4)

            pe.wait_ge(const_step, 2)
            ffn(FFN[0], 0)

            pe.wait_ge(const_step, 14)

            def proj(u, ks, evacs=None, i=0):
                if ks[0] == 0 and evacs is not None:
                    pe.wait_ge(m_evac, evacs + i * 6)
                products(u, (u - MX) % 2, ks, ks, xh, xl, first=ks[0] == 0, last=ks[-1] == KD - 1, i=i, stride=6,
                         inc=unit_done if ks[-1] == KD - 1 else None)

            def head_sum(c, done, i=0, cc=0):
                pe.wait_ge(done, cc)
                pe.matmul(ps[:, BN, :], headones[:, :], sqq[:, :], start=True, stop=True).then_inc(hsum, 1)

            def scores(j, n, z, i=0):
                w = T - P * j
                for h in range(2):
                    rows = slice(HD * h, HD * h + HD)
                    pe.matmul(ps[:, z + h, 0:w], kn[rows, P * j:P * j + P], qn[rows, P * j:T], start=True, stop=False,
                              skip_group_check=True)
                for h in range(2):
                    mm = pe.matmul(ps[:, z + h, 0:P], identb[:, :], blocked[:, :], start=False, stop=False,
                                   skip_group_check=True)
                mm.then_inc(z_ready, 1)

            def minus_later(j, n, z, i=0):
                pe.wait_ge(sp_done, n + 1 + i)
                for h in range(2):
                    mm = pe.matmul(ps[:, z + h, 0:T - P * j], negtri[:, :], sp_[j][:, h, :], start=False, stop=j == QB - 1,
                                   skip_group_check=True)
                    for jj in range(j + 1, QB):
                        mm = pe.matmul(ps[:, z + h, P * (jj - j):T - P * j], negones[:, :], sp_[jj][:, h, :], start=False,
                                       stop=jj == QB - 1, skip_group_check=True)
                mm.then_inc(later_done, 1)

            def values(j, n, i=0):
                pe.wait_ge(a_done, n + 1 + i)
                for h in range(2):
                    rows = slice(HD * h, HD * h + HD)
                    mm = pe.matmul(ps[rows, BO, P * j:T], vtok[:, j, rows], att[j][:, h, :], start=j == QB - 1, stop=j == 0,
                                   skip_group_check=True)
                return mm

            ready = (xl_done, xl_before[1])
            pe.wait_ge(x_new, X_AT[2] - 1)
            products(MX, 0, K8, K8, xh, xl, ready, i=0)
            sum_squares(1)
            pe.wait_ge(x_new, X_AT[2])
            products(MX + 1, 1, K8, K8, xh, xl)
            proj(MX + 2, range(4), 1)
            pe.wait_ge(var_done, 2)
            head_sum(0, q_sq, cc=1)
            proj(MX + 2, range(4, 8))

            def pair(i, last):
                c = CT - 1 if last else 0
                one = 0 if last else i
                i2, i4 = one * 2, one * 4
                B = MX + 3 + 6 * c
                E = 3 + 6 * c

                def part(local, ks):
                    proj(B + local, ks, E + local - 1, one)
                A, Z, ALL = range(4), range(4, 8), range(8)
                part(0, A)
                pe.wait_ge(hvar, 2 * c + 1 + i2)
                head_sum(2 * c + 1, k_sq, cc=c + 1 + one)
                part(0, Z)
                pe.wait_ge(m_evac, E + one * 6)
                pe.wait_ge(hvar, 2 * c + 2 + i2)
                for b in range(QB):
                    mm = pe.transpose(ps[:, BN, P * b:P * b + P], vt[:, P * b:P * b + P], ident[:, :])
                mm.then_inc(v_turned, 1)
                part(1, A)
                pe.wait_ge(qk_ready, 2 * c + 2 + i2)
                scores(3, 0, ZA)
                scores(2, 0, ZB)
                part(1, Z)
                part(2, ALL)
                minus_later(3, 4 * c, ZA, i4)
                minus_later(2, 4 * c + 1, ZB, i4)
                if last:
                    wo_tile(0, ych, ycl)
                    wo_tile(1, ych, ycl)
                else:
                    part(3, A)
                pe.wait_ge(v_ready, c + 1 + one)
                pe.wait_ge(o_free, c + 1 + one)
                values(3, 4 * c, i4)
                values(2, 4 * c + 1, i4)
                scores(1, 0, ZA)
                scores(0, 0, ZB)
                if last:
                    for m in range(2, 6):
                        wo_tile(m, ych, ycl)
                else:
                    part(3, Z)
                    part(4, A)
                    pe.wait_ge(v_ready, 1 + one)
                    head_sum(2, q_sq, cc=2 + one)
                    part(4, Z)
                    part(5, A)
                minus_later(1, 4 * c + 2, ZA, i4)
                minus_later(0, 4 * c + 3, ZB, i4)
                if last:
                    wo_tile(6, ych, ycl)
                else:
                    part(5, Z)
                values(1, 4 * c + 2, i4)
                values(0, 4 * c + 3, i4).then_inc(o_done, 1)

            def wo_tile(m, mh, ml):
                conv_half = mh is ych
                half = m if conv_half else KD + m
                if half < 2:
                    pe.wait_ge(m_evac, N_IN - 1 + m)
                elif half < KD + 2:
                    pe.wait_ge(wo_evac, half - 1)
                else:
                    pe.wait_ge(x_new, X_AT[2] + m - 1)
                u, odd = WO + half // 2, m % 2
                ready = (yc_done, 2 * CT - 4) if conv_half else (o_free, CT + 1 - 4)
                b = u % 2
                pe.wait_ge(lo_done, u + 1)
                for k in range(4):
                    if k == 3:
                        pe.wait_ge(ready[0], ready[1] + 4)
                    a = 4 * odd + k
                    w_hi, w_lo = wh[:, b, a * P:(a + 1) * P], wl[:, b, a * P:(a + 1) * P]
                    pe.matmul(ps[:, odd, :], w_hi, mh[:, k, :], start=k == 0, stop=False)
                    pe.matmul(ps[:, odd, :], w_hi, ml[:, k, :], start=False, stop=False)
                    mm = pe.matmul(ps[:, odd, :], w_lo, mh[:, k, :], start=False, stop=k == 3)
                mm.then_inc(wo_even if not odd else unit_done, 1)

            with pe.Fori(0, CT - 1) as i:
                pair(i, False)
            pair(0, True)
            wo_tile(KD - 1, ych, ycl)
            for m in range(KD):
                wo_tile(m, ysh, ysl)
            ffn(FFN[1], 2)

            for m in range(KD):
                b, u = m % 2, PL + m
                if m == 0:
                    pe.wait_ge(x_new, X_LAST - 1)
                elif m == 1:
                    pe.wait_ge(FFN[1]["banks"], 4 + N_GU)
                else:
                    pe.wait_ge(ple_m, m - 1)
                products(u, 2 * b, K8, K8, xh, xl, (xl_done, xl_before[3]) if m == 0 else None, inc=None)
                if m == 0:
                    sum_squares(3)
                    pe.wait_ge(x_new, X_LAST)
                    pe.wait_ge(p_lo, PK)
                products(u, 2 * b + 1, range(PK), range(KD, KD + PK), ph, pl)



def kernel(**inputs):
    import concourse.bacc as bacc
    from concourse.bass_utils import run_bass_kernel_spmd

    a = {name: np.asarray(v) for name, v in inputs.items()}
    rows = np.ascontiguousarray

    def feature_major(t, tiles):
        return rows(t.T.reshape(tiles, P, T).transpose(1, 0, 2))

    def k_tiles(w, k):
        return w.reshape(k, P, w.shape[1] // P, P).transpose(2, 1, 0, 3)

    def gate_up(g, u):
        return rows(np.stack([k_tiles(g, KD), k_tiles(u, KD)], axis=1).reshape(N_GU, P, KD * P))

    def down(w):
        return rows(k_tiles(w, KF).reshape(KD, P, 2, KH * P).transpose(0, 2, 1, 3).reshape(N_DN, P, KH * P))

    groups = k_tiles(a["w_in"][0], KD).reshape(6, CT, P, KD * P)
    order = [(g, 0) for g in (3, 4, 5)]
    for t in range(CT):
        order += [(g, t) for g in (0, 1, 2)]
        if t + 1 < CT:
            order += [(g, t + 1) for g in (3, 4, 5)]
    w_in = np.stack([groups[g, t] for g, t in order])
    w_out = a["w_out"][0].reshape(2, 4, P, 4, 2, P).transpose(0, 3, 2, 4, 1, 5)
    ple = np.concatenate([k_tiles(a["ple_w_gate"][0], KD), k_tiles(a["ple_w_proj"][0], PK)], axis=2)

    def columns(v, n):
        return v.reshape(n, P).T

    norms = [columns(a[n][0], KD) for n in ("ffn1_norm", "mix_norm", "ffn2_norm", "ple_norm")]
    conv_w = a["conv_w"][0].reshape(3, CT, P).transpose(2, 1, 0).reshape(P, 3 * CT)
    heads = [np.concatenate([a[n][0], a[n][0]]).reshape(P, 1) for n in ("q_norm", "k_norm")]
    params = np.concatenate(norms + [conv_w, columns(a["conv_b"][0], CT)] + heads, axis=1)

    arrays = {
        "xT": feature_major(a["x"][0], KD), "pT": feature_major(a["p"][0, 0], PK), "params": rows(params),
        "gu1": gate_up(a["ffn1_w_gate"][0], a["ffn1_w_up"][0]), "dn1": down(a["ffn1_w_down"][0]),
        "w_in": rows(w_in), "w_out": rows(w_out.reshape(N_WO, P, KD * P)),
        "gu2": gate_up(a["ffn2_w_gate"][0], a["ffn2_w_up"][0]), "dn2": down(a["ffn2_w_down"][0]),
        "ple": rows(ple.reshape(KD, P, (KD + PK) * P)),
    }
    nc = bacc.Bacc("TRN2", target_bir_lowering=False, num_devices=1)
    args = [nc.dram_tensor(name, v.shape, mybir.dt.from_np(v.dtype), kind="ExternalInput").ap()
            for name, v in arrays.items()]
    args.append(nc.dram_tensor("outT", (P, KD, T), F32, kind="ExternalOutput").ap())
    build(nc, *args)
    r = run_bass_kernel_spmd(nc, [arrays], core_ids=[0])
    out = r.results[0]["outT"]
    return rows(out.transpose(2, 1, 0).reshape(1, T, D))
```

```python
from contextlib import ExitStack

import numpy as np

import concourse.bass as bass
from concourse import mybir

F32 = mybir.dt.float32
F32R = mybir.dt.float32r
BF16 = mybir.dt.bfloat16
ACT = mybir.ActivationFunctionType
ALU = mybir.AluOpType

P = 128
T = 512
D = 1024
KD = D // P
F = 2816
KF = F // P
KH = KF // 2
PK = 256 // P
CT = 4
HD = 64
OWN = [slice(0, HD), slice(HD, P)]
QB = T // P
EPS = 1e-6
BLOCKED = -1e30

N_GU = 2 * KF
N_DN = 2 * KD
N_IN = 6 * CT
N_WO = 8
F1, D1 = 0, N_GU
MX = D1 + N_DN
WO = MX + N_IN
F2 = WO + N_WO
D2 = F2 + N_GU
PL = D2 + N_DN
UNITS = PL + KD
RAW = 4
POOL_SQ = 3


def raw_plan():
    slot = [u % 2 if MX <= u < WO else u % RAW for u in range(UNITS)]
    fills, previous, last = [], [], {}
    for u, s in enumerate(slot):
        previous.append(last.get(s))
        last[s] = u
        fills.append(slot[:u + 1].count(s))
    return slot, fills, previous


SLOT, FILLS, PREVIOUS = raw_plan()


def along(table, u, stride, n):
    step = table[u + stride] - table[u] if n > 1 else 0
    assert all(table[u + i * stride] == table[u] + i * step for i in range(n))
    return table[u], step


def build(nc, xT, pT, params, gu1, dn1, w_in, w_out, gu2, dn2, ple, outT):
    ctx = ExitStack()
    with ctx:
        def sb(name, shape, dt=F32, stack=None):
            return (stack or ctx).enter_context(nc.sbuf_tensor(name, shape, dt))

        def sem(name):
            return ctx.enter_context(nc.semaphore(name))

        x = sb("x", [P, KD, T])
        xh = sb("xh", [P, KD, T], F32R)
        xl = sb("xl", [P, KD, T], F32R)
        raw = sb("raw", [P, RAW, KH * P])
        wh = sb("wh", [P, 2, KH * P], F32R)
        wl = sb("wl", [P, 2, KH * P], F32R)
        rms = sb("rms", [P, T])
        sqacc = sb("sqacc", [P, T])
        sq = sb("sq", [P, 2, T])
        sqh, sql = sb("sqh", [P, T], F32R), sb("sql", [P, T], F32R)
        y0 = sb("y0", [P, T])
        par = sb("par", [P, 50])
        one_col = sb("one_col", [P, 1])
        ones = sb("ones", [P, P], F32R)
        headones = sb("headones", [P, P], F32R)
        ones_f = sb("ones_f", [P, P])
        headones_f = sb("headones_f", [P, P])
        tri_f = sb("tri_f", [P, P])
        minus_f = sb("minus_f", [P, P])
        negtri = sb("negtri", [P, P], F32R)
        negones = sb("negones", [P, P], F32R)
        eps_col = sb("eps_col", [P, 1])
        ident = sb("ident", [P, P])
        identb = sb("identb", [P, P], BF16)
        blocked = sb("blocked", [P, P], BF16)
        gq8 = sb("gq8", [P, 1])
        pad = sb("pad", [P, 4])
        act_in = sb("act_in", [P, 2, T])
        upr = sb("upr", [P, T])
        hid = sb("hid", [P, T])
        pool_sq = [y0, upr, hid]
        var, nw = upr, hid
        praw = act_in
        ffn_only = ExitStack()
        hh = sb("hh", [P, KF, T], F32R, ffn_only)
        hl = sb("hl", [P, KF, T], F32R, ffn_only)
        ffn_only.close()
        mix_only = ExitStack()
        qt = sb("qt", [P, T], F32, mix_only)
        kt = sb("kt", [P, T], F32, mix_only)
        vt = sb("vt", [P, T], F32, mix_only)
        qhh = [sb(f"qhh{h}", [P, T], F32R, mix_only) for h in range(2)]
        ql = sb("ql", [P, T], F32R, mix_only)
        khl = [sb(f"khl{h}", [P, T], F32R, mix_only) for h in range(2)]
        vtok = sb("vtok", [P, QB, P], F32, mix_only)
        bt = sb("bt", [P, T], F32, mix_only)
        cgate = sb("cgate", [P, T], F32, mix_only)
        ut = sb("ut", [P, T], F32, mix_only)
        yq = sb("yq", [P, T], F32, mix_only)
        att = [sb(f"att{j}", [P, 2, T - P * j], F32, mix_only) for j in range(QB)]
        sph = [sb(f"sph{j}", [P, 2, T - P * j], F32R, mix_only) for j in range(QB)]
        spl = [sb(f"spl{j}", [P, 2, T - P * j], F32R, mix_only) for j in range(QB)]
        yh = sb("yh", [P, KD, T], F32R, mix_only)
        yl = sb("yl", [P, KD, T], F32R, mix_only)
        mix_only.close()
        ple_only = ExitStack()
        ph = sb("ph", [P, PK, T], F32R, ple_only)
        pl = sb("pl", [P, PK, T], F32R, ple_only)
        ple_only.close()

        ps = ctx.enter_context(nc.psum_tensor("ps", [P, 8, T], F32))
        ZA, ZB, BO, BN = 2, 4, 6, 7

        raw_in = [sem(f"raw_in{s}") for s in range(RAW)]
        hi_done, lo_done, unit_done = sem("hi_done"), sem("lo_done"), sem("unit_done")
        x_in = [sem(f"x_in{c}") for c in range(KD // 2)]
        first_in, first_hi, first_lo = sem("first_in"), sem("first_hi"), sem("first_lo")
        par_in, p_in, gq_ok = sem("par_in"), sem("p_in"), sem("gq_ok")
        const_step = sem("const_step")
        x_new, xh_done, xl_done = sem("x_new"), sem("xh_done"), sem("xl_done")
        sq_done, acc_done = sem("sq_done"), sem("acc_done")
        pool_sq_done = sem("pool_sq_done")
        sum_hi, sum_lo = sem("sum_hi"), sem("sum_lo")
        sum_done, var_done, guess_done = sem("sum_done"), sem("var_done"), sem("guess_done")
        newton, rms_done, ln_done = sem("newton"), sem("rms_done"), sem("ln_done")
        out_ready, stored = sem("out_ready"), sem("stored")

        g_col = lambda n, k: par[:, 8 * n + k:8 * n + k + 1]
        conv_w = lambda t, tap: par[:, 32 + 3 * t + tap:33 + 3 * t + tap]
        conv_b = lambda t: par[:, 44 + t:45 + t]
        gq, gk = par[:, 48:49], par[:, 49:50]

        block = ctx.enter_context(nc.Block())

        FFN = []
        for n, (u0, d0) in enumerate(((F1, D1), (F2, D2))):
            FFN.append(dict(
                n=n, u0=u0, d0=d0,
                banks=sem(f"ffn{n}_banks"), silu=sem(f"ffn{n}_silu"), hid=sem(f"ffn{n}_hid"),
                hh=sem(f"ffn{n}_hh"), hl=sem(f"ffn{n}_hl")))
        m_evac = sem("mix_evac")
        head_sq, head_sq_hi, head_sq_lo = sem("head_sq"), sem("head_sq_hi"), sem("head_sq_lo")
        hsum, hln, hguess = sem("hsum"), sem("hln"), sem("hguess")
        qk_normed, qk_hi, qk_lo = sem("qk_normed"), sem("qk_hi"), sem("qk_lo")
        q_twice = sem("q_twice")
        v_turned, v_ready = sem("v_turned"), sem("v_ready")
        z_ready, abs_done, e_done, l_done = (sem(s) for s in ("z_ready", "abs_done", "e_done", "l_done"))
        sp_done, sp_hi, sp_lo = sem("sp_done"), sem("sp_hi"), sem("sp_lo")
        later_done, a_done = sem("later_done"), sem("a_done")
        o_done, o_hi, o_free = sem("o_done"), sem("o_hi"), sem("o_free")
        conv = sem("conv_step")
        yc_done = sem("yc_done")
        wo_evac, wo_even = sem("wo_evac"), sem("wo_even")
        ple_gate = sem("ple_gate")
        ple_t, ple_s, ple_m, p_hi, p_lo = (sem(s) for s in ("ple_t", "ple_s", "ple_m", "p_hi", "p_lo"))

        NORM1, NORMX, NORM2, NORMP = range(4)
        xl_before = [8 * n for n in range(5)]
        X_AT = [None, 2, 2 + KD, 2 + 2 * KD]
        X_LAST = 2 + 3 * KD
        CONV_LAST, HEADS_FIRST, HEADS_LAST = 2 * CT - 2, CT - 1, 2 * CT - 1

        @block.sync
        def _(sp):
            def load(src, u, nk, i=0, stride=0, n=1):
                if PREVIOUS[u] is not None:
                    a, b = along(PREVIOUS, u, stride, n)
                    sp.wait_ge(lo_done, a + 1 + i * b)
                sp.dma_start(raw[:, SLOT[u], 0:nk * P], src).then_inc(raw_in[SLOT[u]], 16)

            sp.dma_start(par[:, :], params[:, :]).then_inc(par_in, 16)
            half = KD * P // 2
            sp.dma_start(raw[:, 0, 0:half], gu1[0, :, 0:half]).then_inc(first_in, 16)
            for c in range(KD // 2):
                sp.dma_start(x[:, 2 * c:2 * c + 2, :], xT[:, 2 * c:2 * c + 2, :]).then_inc(x_in[c], 16)
                if c == 0:
                    sp.dma_start(raw[:, 0, half:2 * half], gu1[0, :, half:2 * half]).then_inc(raw_in[0], 16)
            load(gu1[1], F1 + 1, KD)

            def ffn_loads(ff, gu, dn, done):
                for u in range(done, RAW):
                    load(gu[u], ff["u0"] + u, KD)
                n = N_GU // RAW - 1
                with sp.Fori(0, n) as i:
                    for j in range(RAW):
                        load(gu[bass.ds(i * RAW + RAW + j, 1)].rearrange("a p n -> (a p) n"),
                             ff["u0"] + RAW + j, KD, i, RAW, n)
                n = N_DN // RAW
                with sp.Fori(0, n) as i:
                    for j in range(RAW):
                        load(dn[bass.ds(i * RAW + j, 1)].rearrange("a p n -> (a p) n"),
                             ff["d0"] + j, KH, i, RAW, n)

            ffn_loads(FFN[0], gu1, dn1, 2)
            for u in range(3):
                load(w_in[u], MX + u, KD)
            with sp.Fori(0, CT - 1) as i:
                for j in range(6):
                    load(w_in[bass.ds(i * 6 + 3 + j, 1)].rearrange("a p n -> (a p) n"),
                         MX + 3 + j, KD, i, 6, CT - 1)
            for u in range(N_IN - 3, N_IN):
                load(w_in[u], MX + u, KD)
            for u in range(N_WO):
                load(w_out[u], WO + u, KD)
            ffn_loads(FFN[1], gu2, dn2, 0)
            sp.wait_ge(FFN[1]["hid"], KF)
            sp.dma_start(praw[:, :, :], pT[:, :, :]).then_inc(p_in, 16)
            for u in range(KD):
                load(ple[u], PL + u, KD + PK)
            for m in range(KD):
                sp.wait_ge(out_ready, m + 1)
                sp.dma_start(outT[:, m, :], x[:, m, :]).then_inc(stored, 16)
            sp.wait_ge(stored, 16 * KD)

        @block.gpsimd
        def _(pool):
            def select(t, op, base, pattern, mult, fill, step):
                pool.wait_ge(const_step, step)
                pool.affine_select(out=t, in_=t, compare_op=op, fill=fill, base=base, pattern=pattern,
                                   channel_multiplier=mult).then_inc(const_step, 1)

            pool.memset(one_col[:, :], 1.0).then_inc(const_step, 1)
            pool.memset(ones_f[:, :], 1.0).then_inc(const_step, 1)
            pool.memset(eps_col[:, :], EPS).then_inc(const_step, 1)

            def lo(u, nk, i=0, stride=0):
                pool.wait_ge(hi_done, u + 1 + i * stride)
                pool.tensor_tensor(wl[:, u % 2, 0:nk * P], raw[:, SLOT[u], 0:nk * P],
                                   wh[:, u % 2, 0:nk * P].bitcast(F32), ALU.subtract).then_inc(lo_done, 1)

            pool.wait_ge(const_step, 3)
            pool.tensor_copy(ones[:, :], ones_f[:, :]).then_inc(const_step, 1)

            half = KD * P // 2
            pool.wait_ge(first_hi, 1)
            pool.tensor_tensor(wl[:, 0, 0:half], raw[:, 0, 0:half], wh[:, 0, 0:half].bitcast(F32),
                               ALU.subtract).then_inc(first_lo, 1)
            pool.wait_ge(hi_done, 1)
            pool.tensor_tensor(wl[:, 0, half:2 * half], raw[:, 0, half:2 * half],
                               wh[:, 0, half:2 * half].bitcast(F32), ALU.subtract).then_inc(lo_done, 1)
            for k in range(POOL_SQ):
                pool.wait_ge(x_in[k // 2], 16)
                pool.tensor_tensor(pool_sq[k][:, :], x[:, k, :], x[:, k, :], ALU.mult).then_inc(pool_sq_done, 1)
            lo(F1 + 1, KD)
            lo(F1 + 2, KD)
            fills = [(headones_f, 1.0), (tri_f, -1.0), (minus_f, -1.0), (ident, 0.0), (identb, 0.0), (blocked, 0.0)]
            for t, v in fills:
                pool.memset(t[:, :], v).then_inc(const_step, 1)
            n = 4 + len(fills)
            select(headones_f[:, 0:HD], ALU.is_ge, HD - 1, [[0, HD]], -1, 0.0, n)
            select(headones_f[:, HD:P], ALU.is_ge, -HD, [[0, HD]], 1, 0.0, n)
            select(tri_f[:, :], ALU.is_ge, 0, [[-1, P]], 1, 0.0, n)
            select(ident[:, :], ALU.not_equal, 0, [[-1, P]], 1, 1.0, n)
            select(identb[:, :], ALU.not_equal, 0, [[-1, P]], 1, 1.0, n)
            select(blocked[:, :], ALU.is_gt, 0, [[1, P]], -1, BLOCKED, n)

            pool.wait_ge(const_step, n + 6)
            pool.tensor_copy(negtri[:, :], tri_f[:, :]).then_inc(const_step, 1)
            pool.tensor_copy(negones[:, :], minus_f[:, :]).then_inc(const_step, 1)
            pool.tensor_copy(headones[:, :], headones_f[:, :]).then_inc(const_step, 1)

            def ffn(ff, first):
                u0, d0 = ff["u0"], ff["d0"]
                for u in range(first, RAW):
                    lo(u0 + u, KD)
                with pool.Fori(0, N_GU // RAW - 1) as i:
                    for j in range(RAW):
                        lo(u0 + RAW + j, KD, i, RAW)
                with pool.Fori(0, N_DN // RAW) as i:
                    for j in range(RAW):
                        lo(d0 + j, KH, i, RAW)

            ffn(FFN[0], 3)
            for u in range(MX, MX + 3):
                lo(u, KD)
            with pool.Fori(0, CT - 1) as i:
                for j in range(6):
                    lo(MX + 3 + j, KD, i, 6)
            for u in range(MX + N_IN - 3, F2):
                lo(u, KD)
            ffn(FFN[1], 0)
            for u in range(PL, UNITS):
                lo(u, KD + PK)

        @block.scalar
        def _(act):
            def hi(u, nk, i=0, stride=0, n=1):
                a, b = along(FILLS, u, stride, n)
                act.wait_ge(raw_in[SLOT[u]], 16 * a + i * (16 * b))
                if u >= 2:
                    act.wait_ge(unit_done, u - 1 + i * stride)
                act.activation(wh[:, u % 2, 0:nk * P], raw[:, SLOT[u], 0:nk * P], ACT.Copy).then_inc(hi_done, 1)

            def guess(norm):
                act.preload_act_table_set("natural_log_exp_and_others")
                act.wait_ge(var_done, norm + 1)
                act.activation(y0[:, :], var[:, :], ACT.Ln).then_inc(ln_done, 1)
                act.wait_ge(ln_done, norm + 1)
                act.activation(y0[:, :], y0[:, :], ACT.Exp, scale=-0.5).then_inc(guess_done, 1)

            half = KD * P // 2
            act.wait_ge(first_in, 16)
            act.activation(wh[:, 0, 0:half], raw[:, 0, 0:half], ACT.Copy).then_inc(first_hi, 1)
            act.wait_ge(par_in, 16)
            for k in range(KD):
                act.wait_ge(x_in[k // 2], 16)
                act.activation(xh[:, k, :], x[:, k, :], ACT.Identity, scale=g_col(NORM1, k)).then_inc(xh_done, 1)
                if k == 1:
                    act.wait_ge(raw_in[0], 16)
                    act.activation(wh[:, 0, half:2 * half], raw[:, 0, half:2 * half], ACT.Copy).then_inc(hi_done, 1)
            hi(F1 + 1, KD)
            for k in range(POOL_SQ, KD):
                act.wait_ge(acc_done, k)
                act.activation(sq[:, k % 2, :], x[:, k, :], ACT.Square).then_inc(sq_done, 1)
                if k == 5:
                    hi(F1 + 2, KD)

            def new_x(norm, m, b, i=0, step=0):
                act.wait_ge(x_new, X_AT[norm] + m + 1 + i * step)
                act.wait_ge(acc_done, 9 * norm + m + i * step)
                if step:
                    act.nop(nofuse=True)
                    xm = x[:, bass.ds(i * step + m, 1), :]
                    dst = xh[:, bass.ds(i * step + m, 1), :]
                    gain = par[:, bass.ds(i * step + m + 8 * norm, 1)]
                else:
                    xm, dst, gain = x[:, m, :], xh[:, m, :], g_col(norm, m)
                act.activation(dst, xm, ACT.Identity, scale=gain).then_inc(xh_done, 1)
                act.activation(sq[:, b, :], xm, ACT.Square).then_inc(sq_done, 1)

            def ffn(ff, nxt, nxt_nk, norm):
                u0, d0 = ff["u0"], ff["d0"]

                def silu(f, b, i=0, step=0):
                    act.wait_ge(ff["banks"], 4 + 2 * f + 1 + i * 2 * step)
                    act.activation(act_in[:, b, :], act_in[:, b, :], ACT.Silu).then_inc(ff["silu"], 1)

                if norm > 1:
                    hi(u0 + 2, KD)
                guess(norm - 1)
                hi(u0 + 3, KD)
                silu(0, 0)
                hi(u0 + 4, KD)
                silu(1, 1)
                hi(u0 + 5, KD)
                n = N_GU // RAW - 2
                with act.Fori(0, n) as i:
                    hi(u0 + 6, KD, i, 4, n)
                    silu(2, 0, i, 2)
                    hi(u0 + 7, KD, i, 4, n)
                    hi(u0 + 8, KD, i, 4, n)
                    silu(3, 1, i, 2)
                    hi(u0 + 9, KD, i, 4, n)
                hi(u0 + N_GU - 2, KD)
                silu(KF - 2, 0)
                hi(u0 + N_GU - 1, KD)
                hi(d0, KH)
                silu(KF - 1, 1)
                hi(d0 + 1, KH)
                n = KD // 2 - 1
                with act.Fori(0, n) as i:
                    for j in range(2):
                        hi(d0 + 2 + 2 * j, KH, i, 4, n)
                        hi(d0 + 3 + 2 * j, KH, i, 4, n)
                        new_x(norm, j, j, i, 2)
                for m in range(KD - 2, KD):
                    for e in range(2):
                        u = d0 + 2 * m + 2 + e
                        if u < d0 + N_DN:
                            hi(u, KH)
                        else:
                            hi(nxt + u - d0 - N_DN, nxt_nk)
                    new_x(norm, m, m % 2)

            ffn(FFN[0], MX, KD, 1)

            def head_guess(c, i=0):
                act.wait_ge(hsum, c + 1 + i)
                if c or not isinstance(i, int):
                    act.wait_ge(qk_normed, c + i)
                act.activation(yq[:, :], ps[:, BN, :], ACT.Ln, scale=1.0 / HD, bias=eps_col[:, :]).then_inc(hln, 1)
                act.wait_ge(hln, c + 1 + i)
                act.activation(yq[:, :], yq[:, :], ACT.Exp, scale=-0.5).then_inc(hguess, 1)

            def softplus(j, n, z, i=0):
                act.wait_ge(z_ready, n + 1 + i)
                act.activation(att[j][:, :, :], ps[:, z:z + 2, 0:T - P * j], ACT.Abs).then_inc(abs_done, 1)
                act.wait_ge(abs_done, n + 1 + i)
                act.activation(att[j][:, :, :], att[j][:, :, :], ACT.Exp, scale=-1.0).then_inc(e_done, 1)
                act.wait_ge(e_done, n + 1 + i)
                act.activation(att[j][:, :, :], att[j][:, :, :], ACT.Ln, bias=one_col[:, :]).then_inc(l_done, 1)

            def weights(j, n, z, i=0):
                act.wait_ge(later_done, n + 1 + i)
                w = T - P * j
                act.activation(att[j][:, :, :], ps[:, z:z + 2, 0:w], ACT.Exp).then_inc(a_done, 1)

            def head_square(t, evac, i=0, count=None):
                act.wait_ge(m_evac, evac + i * 6)
                if count is not None:
                    act.wait_ge(hsum, count + i * 2)
                act.activation(sqh[:, :], t[:, :], ACT.Square).then_inc(head_sq_hi, 1)
                act.activation(sq[:, 0, :], t[:, :], ACT.Square).then_inc(head_sq, 1)

            def v_copy(c, i=0):
                act.wait_ge(v_turned, c + 1 + i)
                act.activation(vtok[:, :, :], ps[:, BN, :].rearrange("p (b d) -> p b d", b=QB), ACT.Copy).then_inc(v_ready, 1)

            def out_hi(c, i=None):
                act.wait_ge(o_done, (c if i is None else i) + 1)
                if i is None:
                    dst, src = yh[:, HEADS_LAST, :], ps[:, BO, :]
                else:
                    act.nop(nofuse=True)
                    dst, src = yh[:, bass.ds(i + HEADS_FIRST, 1), :], ps[:, BO:BO + 1, :]
                act.activation(dst, src, ACT.Copy).then_inc(o_hi, 1)

            hi(MX + 2, KD)
            guess(1)
            head_square(qt, 1)
            hi(MX + 3, KD)
            head_guess(0)
            head_square(kt, 2, count=1)
            hi(MX + 4, KD)

            def pair(i, last):
                i4, i2, i6 = i * 4, i * 2, i * 6
                c = 0 if not last else CT - 1
                if last:
                    i4 = i2 = i6 = 0
                one = i if not last else 0
                b4, b2, b6 = 4 * c, 2 * c, 6 * c
                B = MX + 3 + b6
                n = CT - 1

                def hi6(local):
                    if last:
                        hi(B + local, KD)
                    else:
                        hi(B + local, KD, i, 6, n)
                head_guess(b2 + 1, i2)
                hi6(2)
                v_copy(c, one)
                softplus(3, b4, ZA, i4)
                softplus(2, b4 + 1, ZB, i4)
                hi6(3)
                hi6(4)
                weights(3, b4, ZA, i4)
                weights(2, b4 + 1, ZB, i4)
                softplus(1, b4 + 2, ZA, i4)
                hi6(5)
                if not last:
                    head_square(qt, 7, i, 2)
                softplus(0, b4 + 3, ZB, i4)
                if not last:
                    head_guess(2, i2)
                    head_square(kt, 8, i, 3)
                hi6(6)
                if last:
                    hi6(7)
                weights(1, b4 + 2, ZA, i4)
                weights(0, b4 + 3, ZB, i4)
                if not last:
                    hi6(7)
                    out_hi(0, i)
                else:
                    out_hi(CT - 1)

            with act.Fori(0, CT - 1) as i:
                pair(i, False)
            pair(0, True)
            hi(WO + 5, KD)
            for n in range(4):
                new_x(2, 2 * n, 0)
                hi(WO + 6 + n, KD)
                new_x(2, 2 * n + 1, 1)
            ffn(FFN[1], PL, KD + PK, 3)

            for k in range(PK):
                act.wait_ge(p_in, 16)
                act.activation(ph[:, k, :], praw[:, k, :], ACT.Copy).then_inc(p_hi, 1)
            hi(PL + 2, KD + PK)
            guess(3)
            for m in range(KD):
                if 3 <= m + 2 < KD:
                    hi(PL + m + 2, KD + PK)
                act.wait_ge(ple_t, m + 1)
                act.activation(act_in[:, m % 2, :], act_in[:, m % 2, :], ACT.Sigmoid).then_inc(ple_s, 1)

        @block.vector
        def _(dve):
            def sharpen(count, v, y, t, dst, name, done, i=0):
                dve.scalar_tensor_tensor(t[:, :], y[:, :], -0.5, y[:, :], ALU.mult, ALU.mult).then_inc(name, 1)
                dve.wait_ge(name, 2 * count + 1 + i * 2)
                dve.tensor_tensor(t[:, :], t[:, :], v[:, :], ALU.mult).then_inc(name, 1)
                dve.wait_ge(name, 2 * count + 2 + i * 2)
                dve.scalar_tensor_tensor(dst[:, :], t[:, :], 1.5, y[:, :], ALU.add, ALU.mult).then_inc(done, 1)

            def rms_factor(norm):
                dve.wait_ge(sum_done, norm + 1)
                dve.tensor_scalar(var[:, :], ps[:, BN, :], 1.0 / D, EPS, ALU.mult, ALU.add).then_inc(var_done, 1)
                dve.wait_ge(guess_done, norm + 1)
                sharpen(norm, var, y0, nw, rms, newton, rms_done)
                dve.wait_ge(rms_done, norm + 1)

            dve.memset(pad[:, 0:1], 0.0).then_inc(x_new, 2)
            dve.memset(pad[:, 1:2], 0.0).then_inc(FFN[0]["banks"], 4)
            dve.memset(pad[:, 2:3], 0.0).then_inc(FFN[1]["banks"], 4)
            dve.memset(pad[:, 3:4], 0.0).then_inc(o_free, 1)
            dve.wait_ge(par_in, 16)
            dve.tensor_scalar(gq8[:, :], gq, HD ** -0.5, None, ALU.mult).then_inc(gq_ok, 1)
            def new_sum(norm):
                dve.memset(sqacc[:, :], 0.0).then_inc(acc_done, 1)

            def add_square(norm, m, b, i=0, step=0):
                dve.wait_ge(sq_done, 8 * norm + m + 1 - POOL_SQ + i * step)
                dve.wait_ge(acc_done, 9 * norm + m + 1 + i * step)
                dve.tensor_tensor(sqacc[:, :], sqacc[:, :], sq[:, b, :], ALU.add).then_inc(acc_done, 1)

            def split_sum(norm):
                dve.wait_ge(acc_done, 9 * (norm + 1))
                dve.tensor_scalar(sqh[:, :], sqacc[:, :], 1.0, None, ALU.mult).then_inc(sum_hi, 1)
                dve.wait_ge(sum_hi, norm + 1)
                dve.tensor_tensor(sql[:, :], sqacc[:, :], sqh[:, :].bitcast(F32), ALU.subtract).then_inc(sum_lo, 1)

            new_sum(0)
            for k in range(KD):
                dve.wait_ge(xh_done, k + 1)
                dve.scalar_tensor_tensor(xl[:, k, :], x[:, k, :], g_col(NORM1, k), xh[:, k, :].bitcast(F32),
                                         ALU.mult, ALU.subtract).then_inc(xl_done, 1)
                if k >= KD - POOL_SQ:
                    n = k - KD + POOL_SQ
                    dve.wait_ge(pool_sq_done, n + 1)
                    dve.wait_ge(acc_done, n + 1)
                    dve.tensor_tensor(sqacc[:, :], sqacc[:, :], pool_sq[n][:, :], ALU.add).then_inc(acc_done, 1)
            for k in range(POOL_SQ, KD):
                add_square(0, k, k % 2)
            split_sum(0)

            def new_x(norm, m, bank, scale, i=0, step=0, add=True):
                if step:
                    at = bass.ds(i * step + m, 1)
                    xm, h, l = x[:, at, :], xh[:, at, :], xl[:, at, :]
                    gain = par[:, bass.ds(i * step + m + 8 * norm, 1)]
                    src = ps[:, bank:bank + 1, :]
                else:
                    xm, h, l, gain, src = x[:, m, :], xh[:, m, :], xl[:, m, :], g_col(norm, m), ps[:, bank, :]
                dve.scalar_tensor_tensor(xm, src, scale, xm, ALU.mult, ALU.add).then_inc(x_new, 1)
                dve.wait_ge(xh_done, 8 * norm + m + 1 + i * step)
                dve.scalar_tensor_tensor(l, xm, gain, h.bitcast(F32), ALU.mult, ALU.subtract).then_inc(xl_done, 1)
                if add:
                    add_square(norm, m, m % 2, i, step)

            def ffn(ff, norm):
                u0, d0 = ff["u0"], ff["d0"]
                rms_factor(norm - 1)
                n = KF // 2
                with dve.Fori(0, n) as i:
                    for b in range(2):
                        dve.wait_ge(unit_done, u0 + 2 * b + 1 + i * 4)
                        dve.tensor_tensor(act_in[:, b, :], ps[:, 2 * b, :], rms[:, :], ALU.mult).then_inc(ff["banks"], 1)
                        dve.wait_ge(unit_done, u0 + 2 * b + 2 + i * 4)
                        dve.tensor_tensor(upr[:, :], ps[:, 2 * b + 1, :], rms[:, :], ALU.mult).then_inc(ff["banks"], 1)
                        dve.wait_ge(ff["banks"], 4 + 2 * b + 2 + i * 4)
                        dve.wait_ge(ff["silu"], b + 1 + i * 2)
                        dve.tensor_tensor(hid[:, :], act_in[:, b, :], upr[:, :], ALU.mult).then_inc(ff["hid"], 1)
                        dve.wait_ge(ff["hid"], b + 1 + i * 2)
                        at = bass.ds(i * 2 + b, 1)
                        dve.tensor_scalar(hh[:, at, :], hid[:, :], 1.0, None, ALU.mult).then_inc(ff["hh"], 1)
                        dve.wait_ge(ff["hh"], b + 1 + i * 2)
                        dve.tensor_tensor(hl[:, at, :], hid[:, :], hh[:, at, :].bitcast(F32), ALU.subtract).then_inc(ff["hl"], 1)
                new_sum(norm)
                with dve.Fori(0, KD // 2) as i:
                    for j in range(2):
                        dve.wait_ge(unit_done, d0 + 2 * j + 2 + i * 4)
                        new_x(norm, j, j, 0.5, i, 2)
                split_sum(norm)

            ffn(FFN[0], 1)

            def evac(dst, unit, bank, i=0):
                dve.wait_ge(unit_done, unit + 1 + i * 6)
                dve.tensor_tensor(dst[:, :], ps[:, bank, :], rms[:, :], ALU.mult).then_inc(m_evac, 1)

            def square_lo(c, i=0):
                dve.wait_ge(head_sq_hi, c + 1 + i)
                dve.wait_ge(head_sq, c + 1 + i)
                dve.tensor_tensor(sql[:, :], sq[:, 0, :], sqh[:, :].bitcast(F32), ALU.subtract).then_inc(head_sq_lo, 1)

            def head_norm(c, t, gain, i=0):
                is_q = t is qt
                dve.wait_ge(hguess, c + 1 + i)
                dve.scalar_tensor_tensor(t[:, :], t[:, :], gain, yq[:, :], ALU.mult, ALU.mult).then_inc(qk_normed, 1)
                dve.wait_ge(qk_normed, c + 1 + i)
                for h in range(2):
                    dst = qhh[h] if is_q else khl[h]
                    dve.tensor_scalar(dst[OWN[h], :], t[OWN[h], :], 1.0, None, ALU.mult).then_inc(qk_hi, 1)
                for h in range(2):
                    hi = qhh[h] if is_q else khl[h]
                    lo = ql[OWN[h], :] if is_q else khl[h][OWN[1 - h], :]
                    dve.wait_ge(qk_hi, 2 * c + 1 + h + i * 2)
                    dve.tensor_tensor(lo, t[OWN[h], :], hi[OWN[h], :].bitcast(F32), ALU.subtract).then_inc(qk_lo, 1)
                if is_q:
                    for h in range(2):
                        dve.tensor_scalar(qhh[h][OWN[1 - h], :], t[OWN[h], :], 1.0, None, ALU.mult).then_inc(q_twice, 1)

            def softplus(j, n, z, i=0):
                dve.wait_ge(l_done, n + 1 + i)
                w = T - P * j
                dve.scalar_tensor_tensor(att[j][:, :, :], ps[:, z:z + 2, 0:w], 0.0, att[j][:, :, :],
                                         ALU.max, ALU.add).then_inc(sp_done, 1)
                dve.wait_ge(sp_done, n + 1 + i)
                dve.tensor_scalar(sph[j][:, :, :], att[j][:, :, :], 1.0, None, ALU.mult).then_inc(sp_hi, 1)
                dve.wait_ge(sp_hi, n + 1 + i)
                dve.tensor_tensor(spl[j][:, :, :], att[j][:, :, :], sph[j][:, :, :].bitcast(F32),
                                  ALU.subtract).then_inc(sp_lo, 1)

            rms_factor(1)
            evac(qt, MX, 0)
            square_lo(0)
            evac(kt, MX + 1, 1)
            dve.wait_ge(gq_ok, 1)
            head_norm(0, qt, gq8[:, :])
            square_lo(1)
            evac(vt, MX + 2, 0)

            def pair(i, last):
                c = CT - 1 if last else 0
                one = 0 if last else i
                i2, i4, i6 = one * 2, one * 4, one
                B = MX + 3 + 6 * c
                n_conv = 5 * c
                i5 = one * 5

                def bank(local):
                    return (3 + local) % 2

                def ev(dst, local):
                    evac(dst, B + local, bank(local), one)
                head_norm(2 * c + 1, kt, gk, i2)
                ev(bt, 0)
                ev(cgate, 1)
                softplus(3, 4 * c, ZA, i4)
                softplus(2, 4 * c + 1, ZB, i4)
                ev(ut, 2)
                dve.wait_ge(m_evac, 6 * c + 6 + (0 if last else i * 6))
                dve.tensor_tensor(cgate[:, :], cgate[:, :], ut[:, :], ALU.mult).then_inc(conv, 1)
                dve.wait_ge(conv, n_conv + 1 + i5)
                if last:
                    w = [conv_w(c, tap) for tap in range(3)]
                    bias = conv_b(c)
                    y_hi, y_lo = yh[:, CONV_LAST, :], yl[:, CONV_LAST, :]
                else:
                    w = [par[:, bass.ds(i * 3 + (32 + tap), 1)] for tap in range(3)]
                    bias = par[:, bass.ds(i + 44, 1)]
                    y_hi, y_lo = yh[:, bass.ds(i, 1), :], yl[:, bass.ds(i, 1), :]
                dve.tensor_scalar(ut[:, :], cgate[:, :], w[2], bias, ALU.mult, ALU.add).then_inc(conv, 1)
                dve.wait_ge(conv, n_conv + 2 + i5)
                dve.scalar_tensor_tensor(ut[:, 1:T], cgate[:, 0:T - 1], w[1], ut[:, 1:T], ALU.mult, ALU.add).then_inc(conv, 1)
                dve.wait_ge(conv, n_conv + 3 + i5)
                dve.scalar_tensor_tensor(ut[:, 2:T], cgate[:, 0:T - 2], w[0], ut[:, 2:T], ALU.mult, ALU.add).then_inc(conv, 1)
                dve.wait_ge(conv, n_conv + 4 + i5)
                dve.tensor_tensor(ut[:, :], ut[:, :], bt[:, :], ALU.mult).then_inc(conv, 1)
                dve.wait_ge(conv, n_conv + 5 + i5)
                dve.tensor_scalar(y_hi, ut[:, :], 1.0, None, ALU.mult).then_inc(yc_done, 1)
                dve.wait_ge(yc_done, 2 * c + 1 + i2)
                dve.tensor_tensor(y_lo, ut[:, :], y_hi.bitcast(F32), ALU.subtract).then_inc(yc_done, 1)
                if last:
                    add_out(0, 0)
                    add_out(1, 1)
                if last:
                    add_out(2, 0)
                else:
                    ev(qt, 3)
                softplus(1, 4 * c + 2, ZA, i4)
                if last:
                    add_out(3, 1)
                else:
                    square_lo(2, i2)
                softplus(0, 4 * c + 3, ZB, i4)
                if not last:
                    ev(kt, 4)
                    head_norm(2, qt, gq8[:, :], i2)
                    square_lo(3, i2)
                    dve.wait_ge(v_turned, 1 + i)
                    ev(vt, 5)
                    at = bass.ds(i + HEADS_FIRST, 1)
                    dve.wait_ge(o_hi, i + 1)
                    dve.tensor_tensor(yl[:, at, :], ps[:, BO:BO + 1, :], yh[:, at, :].bitcast(F32),
                                      ALU.subtract).then_inc(o_free, 1)
                else:
                    for m in range(4, KD - 1):
                        add_out(m, m % 2)
                    dve.wait_ge(o_hi, CT)
                    dve.tensor_tensor(yl[:, HEADS_LAST, :], ps[:, BO, :], yh[:, HEADS_LAST, :].bitcast(F32),
                                      ALU.subtract).then_inc(o_free, 1)
                    add_out(KD - 1, 1)

            def wo_tile_done(half):
                if half % 2:
                    dve.wait_ge(unit_done, WO + half // 2 + 1)
                else:
                    dve.wait_ge(wo_even, half // 2 + 1)

            def add_out(m, bank):
                wo_tile_done(m)
                dve.tensor_tensor(x[:, m, :], ps[:, bank, :], x[:, m, :], ALU.add).then_inc(wo_evac, 1)

            with dve.Fori(0, CT - 1) as i:
                pair(i, False)
            pair(0, True)
            dve.wait_ge(wo_evac, KD)
            new_sum(2)
            for m in range(KD):
                wo_tile_done(KD + m)
                new_x(2, m, m % 2, 1.0, add=False)
                if m:
                    add_square(2, m - 1, (m - 1) % 2)
            add_square(2, KD - 1, 1)
            split_sum(2)
            ffn(FFN[1], 3)

            for k in range(PK):
                dve.wait_ge(p_hi, k + 1)
                dve.tensor_tensor(pl[:, k, :], praw[:, k, :], ph[:, k, :].bitcast(F32), ALU.subtract).then_inc(p_lo, 1)
            rms_factor(3)
            for m in range(KD):
                b, bank = m % 2, 2 * (m % 3)
                dve.wait_ge(ple_gate, m + 1)
                dve.tensor_tensor(act_in[:, b, :], ps[:, bank, :], rms[:, :], ALU.mult).then_inc(ple_t, 1)
                dve.wait_ge(unit_done, PL + m + 1)
                dve.wait_ge(ple_s, m + 1)
                dve.tensor_tensor(upr[:, :], ps[:, bank + 1, :], act_in[:, b, :], ALU.mult).then_inc(ple_m, 1)
                dve.wait_ge(ple_m, m + 1)
                dve.tensor_tensor(x[:, m, :], x[:, m, :], upr[:, :], ALU.add).then_inc(out_ready, 1)

        @block.tensor
        def _(pe):
            def products(u, bank, ks, at, mh, ml, ready=None, first=True, last=True, i=0, stride=0, inc=unit_done):
                b = u % 2
                w_hi = [wh[:, b, a * P:(a + 1) * P] for a in at]
                w_lo = [wl[:, b, a * P:(a + 1) * P] for a in at]
                pe.wait_ge(*((first_hi, 1) if u == 0 and isinstance(i, int) else (hi_done, u + 1 + i * stride)))
                for n, k in enumerate(ks):
                    if u == 0 and isinstance(i, int) and n == KD // 2:
                        pe.wait_ge(hi_done, 1)
                    if ready is not None:
                        pe.wait_ge(ready[0], ready[1] + k + 1)
                    pe.matmul(ps[:, bank, :], w_hi[n], mh[:, k, :], start=first and n == 0, stop=False)
                    pe.matmul(ps[:, bank, :], w_hi[n], ml[:, k, :], start=False, stop=False)
                pe.wait_ge(lo_done, u + 1 + i * stride)
                for n, k in enumerate(ks):
                    mm = pe.matmul(ps[:, bank, :], w_lo[n], mh[:, k, :], start=False, stop=last and n == len(ks) - 1)
                if inc is not None:
                    mm.then_inc(inc, 1)

            def sum_squares(norm):
                if norm:
                    pe.wait_ge(var_done, norm)
                pe.wait_ge(sum_lo, norm + 1)
                pe.matmul(ps[:, BN, :], ones[:, :], sqh[:, :], start=True, stop=False)
                pe.matmul(ps[:, BN, :], ones[:, :], sql[:, :], start=False, stop=True).then_inc(sum_done, 1)

            K8 = range(KD)

            def with_sum(u, bank, norm, k):
                products(u, bank, range(k), range(k), xh, xl, last=False, inc=None)
                sum_squares(norm)
                products(u, bank, range(k, KD), range(k, KD), xh, xl, first=False)

            def ffn(ff, norm):
                u0, d0 = ff["u0"], ff["d0"]
                ready = (xl_done, xl_before[norm])

                def four(i, base, peeled):
                    for j in range(4):
                        pe.wait_ge(ff["banks"], base + j + 1 + i * 4)
                        if peeled and norm and j < 2:
                            pe.wait_ge(x_new, X_AT[norm + 1] - 1 + j)
                        if peeled and norm and j == 1:
                            with_sum(u0 + j, j, norm, 3)
                        else:
                            products(u0 + base + j, j, K8, K8, xh, xl, ready if j == 0 and peeled else None, i=i, stride=4)
                        if peeled and norm == 0 and j == 1:
                            sum_squares(0)
                four(0, 0, True)
                with pe.Fori(0, N_GU // 4 - 1) as i:
                    four(i, 4, False)
                pe.wait_ge(ff["banks"], 4 + N_GU - 2)
                with pe.Fori(0, KD // 2) as i:
                    for j in range(2):
                        pe.wait_ge(x_new, X_AT[norm + 1] - 1 + j + i * 2)
                        for e in range(2):
                            pe.wait_ge(ff["hl"], KH * (e + 1))
                            products(d0 + 2 * j + e, j, range(e * KH, (e + 1) * KH), range(KH), hh, hl,
                                     first=e == 0, last=e == 1, i=i, stride=4)

            pe.wait_ge(const_step, 4)
            ffn(FFN[0], 0)

            pe.wait_ge(const_step, 19)

            def proj(u, ks, evacs=None, i=0):
                if ks[0] == 0 and evacs is not None:
                    pe.wait_ge(m_evac, evacs + i * 6)
                products(u, (u - MX) % 2, ks, ks, xh, xl, first=ks[0] == 0, last=ks[-1] == KD - 1, i=i, stride=6,
                         inc=unit_done if ks[-1] == KD - 1 else None)

            def head_sum(c, i=0):
                pe.wait_ge(head_sq_lo, c + 1 + i)
                pe.matmul(ps[:, BN, :], headones[:, :], sqh[:, :], start=True, stop=False)
                pe.matmul(ps[:, BN, :], headones[:, :], sql[:, :], start=False, stop=True).then_inc(hsum, 1)

            def scores(j, n, z, i=0):
                w = T - P * j
                for h in range(2):
                    pe.matmul(ps[:, z + h, 0:w], khl[h][:, P * j:P * j + P], qhh[h][:, P * j:T], start=True, stop=False,
                              skip_group_check=True)
                for h in range(2):
                    pe.matmul(ps[:, z + h, 0:w], khl[h][OWN[h], P * j:P * j + P], ql[OWN[h], P * j:T], start=False,
                              stop=False, skip_group_check=True)
                for h in range(2):
                    mm = pe.matmul(ps[:, z + h, 0:P], identb[:, :], blocked[:, :], start=False, stop=False,
                                   skip_group_check=True)
                mm.then_inc(z_ready, 1)

            def minus_later(j, n, z, i=0):
                pe.wait_ge(sp_lo, n + 1 + i)
                for h in range(2):
                    for jj in range(j, QB):
                        for part in (sph, spl):
                            mm = pe.matmul(ps[:, z + h, P * (jj - j):T - P * j], (negtri if jj == j else negones)[:, :],
                                           part[jj][:, h, :], start=False, stop=jj == QB - 1 and part is spl,
                                           skip_group_check=True)
                mm.then_inc(later_done, 1)

            def values(j, n, i=0):
                pe.wait_ge(a_done, n + 1 + i)
                for h in range(2):
                    rows = slice(HD * h, HD * h + HD)
                    mm = pe.matmul(ps[rows, BO, P * j:T], vtok[:, j, rows], att[j][:, h, :], start=j == QB - 1, stop=j == 0,
                                   skip_group_check=True)
                return mm

            ready = (xl_done, xl_before[1])
            pe.wait_ge(x_new, X_AT[2] - 1)
            products(MX, 0, K8, K8, xh, xl, ready, i=0)
            pe.wait_ge(x_new, X_AT[2])
            with_sum(MX + 1, 1, 1, 2)
            proj(MX + 2, range(4), 1)
            pe.wait_ge(var_done, 2)
            head_sum(0)
            proj(MX + 2, range(4, 8))

            def pair(i, last):
                c = CT - 1 if last else 0
                one = 0 if last else i
                i2, i4 = one * 2, one * 4
                B = MX + 3 + 6 * c
                E = 3 + 6 * c

                def part(local, ks):
                    proj(B + local, ks, E + local - 1, one)
                A, Z, ALL = range(4), range(4, 8), range(8)
                part(0, A)
                pe.wait_ge(hln, 2 * c + 1 + i2)
                head_sum(2 * c + 1, i2)
                part(0, Z)
                pe.wait_ge(m_evac, E + one * 6)
                pe.wait_ge(hln, 2 * c + 2 + i2)
                for b in range(QB):
                    mm = pe.transpose(ps[:, BN, P * b:P * b + P], vt[:, P * b:P * b + P], ident[:, :])
                mm.then_inc(v_turned, 1)
                part(1, A)
                pe.wait_ge(qk_lo, 4 * c + 4 + i4)
                pe.wait_ge(q_twice, 2 * c + 2 + i2)
                scores(3, 0, ZA)
                scores(2, 0, ZB)
                part(1, Z)
                part(2, ALL)
                minus_later(3, 4 * c, ZA, i4)
                minus_later(2, 4 * c + 1, ZB, i4)
                if last:
                    wo_tile(0)
                    wo_tile(1)
                else:
                    part(3, A)
                pe.wait_ge(v_ready, c + 1 + one)
                pe.wait_ge(o_free, c + 1 + one)
                values(3, 4 * c, i4)
                values(2, 4 * c + 1, i4)
                scores(1, 0, ZA)
                scores(0, 0, ZB)
                if last:
                    for m in range(2, 6):
                        wo_tile(m)
                else:
                    part(3, Z)
                    part(4, A)
                    pe.wait_ge(v_ready, 1 + one)
                    part(4, Z)
                    head_sum(2, i2)
                    part(5, A)
                minus_later(1, 4 * c + 2, ZA, i4)
                minus_later(0, 4 * c + 3, ZB, i4)
                if last:
                    wo_tile(6)
                else:
                    part(5, Z)
                values(1, 4 * c + 2, i4)
                values(0, 4 * c + 3, i4).then_inc(o_done, 1)

            def wo_tile(half):
                m, later = half % KD, half // KD
                if half < 2:
                    pe.wait_ge(m_evac, N_IN - 1 + m)
                elif half < KD + 2:
                    pe.wait_ge(wo_evac, half - 1)
                else:
                    pe.wait_ge(x_new, X_AT[2] + m - 1)
                u, odd = WO + half // 2, m % 2
                pe.wait_ge(lo_done, u + 1)
                for k in range(4):
                    if not later and k == 0:
                        pe.wait_ge(yc_done, 2 * (CT - 1))
                        pe.wait_ge(o_free, 2)
                    if later and k == 2:
                        pe.wait_ge(yc_done, 2 * CT)
                    if later and k == 3:
                        pe.wait_ge(o_free, CT + 1)
                    a, y = 4 * odd + k, 4 * later + k
                    w_hi, w_lo = wh[:, u % 2, a * P:(a + 1) * P], wl[:, u % 2, a * P:(a + 1) * P]
                    pe.matmul(ps[:, odd, :], w_hi, yh[:, y, :], start=k == 0, stop=False)
                    pe.matmul(ps[:, odd, :], w_lo, yh[:, y, :], start=False, stop=False)
                    mm = pe.matmul(ps[:, odd, :], w_hi, yl[:, y, :], start=False, stop=k == 3)
                mm.then_inc(wo_even if not odd else unit_done, 1)

            with pe.Fori(0, CT - 1) as i:
                pair(i, False)
            pair(0, True)
            for half in range(KD - 1, 2 * KD):
                wo_tile(half)
            ffn(FFN[1], 2)

            for m in range(KD):
                b, u = m % 3, PL + m
                if m == 0:
                    pe.wait_ge(x_new, X_LAST - 1)
                elif m == 1:
                    pe.wait_ge(FFN[1]["banks"], 4 + N_GU)
                elif m > 2:
                    pe.wait_ge(ple_m, m - 2)
                products(u, 2 * b, K8, K8, xh, xl, (xl_done, xl_before[3]) if m == 0 else None, inc=ple_gate)
                if m == 0:
                    sum_squares(3)
                    pe.wait_ge(x_new, X_LAST)
                    pe.wait_ge(p_lo, PK)
                products(u, 2 * b + 1, range(PK), range(KD, KD + PK), ph, pl)



def kernel(**inputs):
    import concourse.bacc as bacc
    from concourse.bass_utils import run_bass_kernel_spmd

    a = {name: np.asarray(v) for name, v in inputs.items()}
    rows = np.ascontiguousarray

    def feature_major(t, tiles):
        return rows(t.T.reshape(tiles, P, T).transpose(1, 0, 2))

    def k_tiles(w, k):
        return w.reshape(k, P, w.shape[1] // P, P).transpose(2, 1, 0, 3)

    def gate_up(g, u):
        return rows(np.stack([k_tiles(g, KD), k_tiles(u, KD)], axis=1).reshape(N_GU, P, KD * P))

    def down(w):
        return rows(k_tiles(w, KF).reshape(KD, P, 2, KH * P).transpose(0, 2, 1, 3).reshape(N_DN, P, KH * P))

    groups = k_tiles(a["w_in"][0], KD).reshape(6, CT, P, KD * P)
    order = [(g, 0) for g in (3, 4, 5)]
    for t in range(CT):
        order += [(g, t) for g in (0, 1, 2)]
        if t + 1 < CT:
            order += [(g, t + 1) for g in (3, 4, 5)]
    w_in = np.stack([groups[g, t] for g, t in order])
    w_out = a["w_out"][0].reshape(KD, P, D)[[0, 1, 2, 4, 5, 6, 3, 7]]
    w_out = w_out.reshape(2, 4, P, 4, 2, P).transpose(0, 3, 2, 4, 1, 5)
    ple = np.concatenate([k_tiles(a["ple_w_gate"][0], KD), k_tiles(a["ple_w_proj"][0], PK)], axis=2)

    def columns(v, n):
        return v.reshape(n, P).T

    norms = [columns(a[n][0], KD) for n in ("ffn1_norm", "mix_norm", "ffn2_norm", "ple_norm")]
    conv_w = a["conv_w"][0].reshape(3, CT, P).transpose(2, 1, 0).reshape(P, 3 * CT)
    heads = [np.concatenate([a[n][0], a[n][0]]).reshape(P, 1) for n in ("q_norm", "k_norm")]
    params = np.concatenate(norms + [conv_w, columns(a["conv_b"][0], CT)] + heads, axis=1)

    arrays = {
        "xT": feature_major(a["x"][0], KD), "pT": feature_major(a["p"][0, 0], PK), "params": rows(params),
        "gu1": gate_up(a["ffn1_w_gate"][0], a["ffn1_w_up"][0]), "dn1": down(a["ffn1_w_down"][0]),
        "w_in": rows(w_in), "w_out": rows(w_out.reshape(N_WO, P, KD * P)),
        "gu2": gate_up(a["ffn2_w_gate"][0], a["ffn2_w_up"][0]), "dn2": down(a["ffn2_w_down"][0]),
        "ple": rows(ple.reshape(KD, P, (KD + PK) * P)),
    }
    nc = bacc.Bacc("TRN2", target_bir_lowering=False, num_devices=1)
    args = [nc.dram_tensor(name, v.shape, mybir.dt.from_np(v.dtype), kind="ExternalInput").ap()
            for name, v in arrays.items()]
    args.append(nc.dram_tensor("outT", (P, KD, T), F32, kind="ExternalOutput").ap())
    build(nc, *args)
    r = run_bass_kernel_spmd(nc, [arrays], core_ids=[0])
    out = r.results[0]["outT"]
    return rows(out.transpose(2, 1, 0).reshape(1, T, D))
```

```python
from contextlib import ExitStack

import numpy as np

import concourse.bass as bass
from concourse import mybir

F32 = mybir.dt.float32
F32R = mybir.dt.float32r
BF16 = mybir.dt.bfloat16
ACT = mybir.ActivationFunctionType
ALU = mybir.AluOpType

P = 128
T = 512
D = 1024
KD = D // P
F = 2816
KF = F // P
KH = KF // 2
PK = 256 // P
CT = 4
HD = 64
OWN = [slice(0, HD), slice(HD, P)]
QB = T // P
EPS = 1e-6
BLOCKED = -1e30

N_GU = 2 * KF
N_DN = 2 * KD
N_IN = 6 * CT
N_WO = 8
F1, D1 = 0, N_GU
MX = D1 + N_DN
WO = MX + N_IN
F2 = WO + N_WO
D2 = F2 + N_GU
PL = D2 + N_DN
UNITS = PL + KD
RAW = 4
X_PIECES = [(0, 1), (1, 2), (2, 4), (4, 6), (6, 8)]
POOL_SQ = 3


def x_piece(k):
    return next(c for c, (first, end) in enumerate(X_PIECES) if first <= k < end)


def raw_plan():
    slot = [u % 2 if MX <= u < WO else u % RAW for u in range(UNITS)]
    fills, previous, last = [], [], {}
    for u, s in enumerate(slot):
        previous.append(last.get(s))
        last[s] = u
        fills.append(slot[:u + 1].count(s))
    return slot, fills, previous


SLOT, FILLS, PREVIOUS = raw_plan()


def along(table, u, stride, n):
    step = table[u + stride] - table[u] if n > 1 else 0
    assert all(table[u + i * stride] == table[u] + i * step for i in range(n))
    return table[u], step


def build(nc, xT, pT, params, gu1, dn1, w_in, w_out, gu2, dn2, ple, outT):
    ctx = ExitStack()
    with ctx:
        def sb(name, shape, dt=F32, stack=None):
            return (stack or ctx).enter_context(nc.sbuf_tensor(name, shape, dt))

        def sem(name):
            return ctx.enter_context(nc.semaphore(name))

        x = sb("x", [P, KD, T])
        xh = sb("xh", [P, KD, T], F32R)
        xl = sb("xl", [P, KD, T], F32R)
        raw = sb("raw", [P, RAW, KH * P])
        wh = sb("wh", [P, 2, KH * P], F32R)
        wl = sb("wl", [P, 2, KH * P], F32R)
        rms = sb("rms", [P, T])
        sqacc = sb("sqacc", [P, T])
        sq = sb("sq", [P, 2, T])
        sqh, sql = sb("sqh", [P, T], F32R), sb("sql", [P, T], F32R)
        y0 = sb("y0", [P, T])
        par = sb("par", [P, 50])
        one_col = sb("one_col", [P, 1])
        ones = sb("ones", [P, P], F32R)
        headones = sb("headones", [P, P], F32R)
        ones_f = sb("ones_f", [P, P])
        headones_f = sb("headones_f", [P, P])
        tri_f = sb("tri_f", [P, P])
        minus_f = sb("minus_f", [P, P])
        negtri = sb("negtri", [P, P], F32R)
        negones = sb("negones", [P, P], F32R)
        eps_col = sb("eps_col", [P, 1])
        ident = sb("ident", [P, P])
        identb = sb("identb", [P, P], BF16)
        blocked = sb("blocked", [P, 2, P], BF16)
        gq8 = sb("gq8", [P, 1])
        pad = sb("pad", [P, 4])
        act_in = sb("act_in", [P, 2, T])
        upr = sb("upr", [P, T])
        hid = sb("hid", [P, T])
        pool_sq = [y0, upr, hid]
        var, nw = upr, hid
        praw = act_in
        ffn_only = ExitStack()
        hh = sb("hh", [P, KF, T], F32R, ffn_only)
        hl = sb("hl", [P, KF, T], F32R, ffn_only)
        ffn_only.close()
        mix_only = ExitStack()
        qt = sb("qt", [P, T], F32, mix_only)
        kt = sb("kt", [P, T], F32, mix_only)
        vt = sb("vt", [P, T], F32, mix_only)
        qhh = [sb(f"qhh{h}", [P, T], F32R, mix_only) for h in range(2)]
        qll = [sb(f"qll{h}", [P, T], F32R, mix_only) for h in range(2)]
        khl = [sb(f"khl{h}", [P, T], F32R, mix_only) for h in range(2)]
        vtok = sb("vtok", [P, QB, P], F32, mix_only)
        bt, cgate, ut, yq = act_in[:, 0, :], act_in[:, 1, :], upr[:, :], y0[:, :]
        att = [sb(f"att{j}", [P, 2, T - P * j], F32, mix_only) for j in range(QB)]
        sph = [sb(f"sph{j}", [P, 2, T - P * j], F32R, mix_only) for j in range(QB)]
        spl = [sb(f"spl{j}", [P, 2, T - P * j], F32R, mix_only) for j in range(QB)]
        tail_h, tail_l = ([None, sb(f"{name}1", [P, 2, T - P], F32R, mix_only), part[2], part[3]]
                          for name, part in (("tail_h", sph), ("tail_l", spl)))
        weight = [att[0], att[1], sq[:, 1, :].rearrange("p (h w) -> p h w", h=2), att[3]]
        yh = sb("yh", [P, KD, T], F32R, mix_only)
        yl = sb("yl", [P, KD, T], F32R, mix_only)
        mix_only.close()
        ple_only = ExitStack()
        ph = sb("ph", [P, PK, T], F32R, ple_only)
        pl = sb("pl", [P, PK, T], F32R, ple_only)
        ple_only.close()

        ps = ctx.enter_context(nc.psum_tensor("ps", [P, 8, T], F32))
        ZA, ZB, BO, BN = 2, 4, 6, 7

        raw_in = [sem(f"raw_in{s}") for s in range(RAW)]
        hi_done, lo_done, unit_done = sem("hi_done"), sem("lo_done"), sem("unit_done")
        x_in = [sem(f"x_in{c}") for c in range(len(X_PIECES))]
        first_in, first_hi, first_lo = sem("first_in"), sem("first_hi"), sem("first_lo")
        par_in, p_in, gq_ok = sem("par_in"), sem("p_in"), sem("gq_ok")
        const_step = sem("const_step")
        x_new, xh_done, xl_done = sem("x_new"), sem("xh_done"), sem("xl_done")
        sq_done, acc_done = sem("sq_done"), sem("acc_done")
        pool_sq_done = sem("pool_sq_done")
        sum_hi, sum_lo = sem("sum_hi"), sem("sum_lo")
        sum_done, var_done, guess_done = sem("sum_done"), sem("var_done"), sem("guess_done")
        newton, rms_done, ln_done = sem("newton"), sem("rms_done"), sem("ln_done")
        out_ready, stored = sem("out_ready"), sem("stored")

        def z_of(j, z):
            w = T - P * j
            return ps[:, z, 0:2 * w].rearrange("p (h w) -> p h w", h=2) if 2 * w <= T else ps[:, z:z + 2, 0:w]

        g_col = lambda n, k: par[:, 8 * n + k:8 * n + k + 1]
        conv_w = lambda t, tap: par[:, 32 + 3 * t + tap:33 + 3 * t + tap]
        conv_b = lambda t: par[:, 44 + t:45 + t]
        gq, gk = par[:, 48:49], par[:, 49:50]

        block = ctx.enter_context(nc.Block())

        FFN = []
        for n, (u0, d0) in enumerate(((F1, D1), (F2, D2))):
            FFN.append(dict(
                n=n, u0=u0, d0=d0,
                banks=sem(f"ffn{n}_banks"), silu=sem(f"ffn{n}_silu"), hid=sem(f"ffn{n}_hid"),
                hh=sem(f"ffn{n}_hh"), hl=sem(f"ffn{n}_hl")))
        m_evac = sem("mix_evac")
        head_sq, head_sq_hi, head_sq_lo = sem("head_sq"), sem("head_sq_hi"), sem("head_sq_lo")
        hsum, hln, hguess = sem("hsum"), sem("hln"), sem("hguess")
        qk_normed, qk_hi, qk_lo = sem("qk_normed"), sem("qk_hi"), sem("qk_lo")
        q_twice = sem("q_twice")
        v_turned, v_ready = sem("v_turned"), sem("v_ready")
        z_ready, abs_done, e_done, l_done = (sem(s) for s in ("z_ready", "abs_done", "e_done", "l_done"))
        sp_done, sp_hi, sp_lo = sem("sp_done"), sem("sp_hi"), sem("sp_lo")
        tail_sum, tail_hi, tail_lo = sem("tail_sum"), sem("tail_hi"), sem("tail_lo")
        later_done, a_done = sem("later_done"), sem("a_done")
        o_done, o_hi, o_free = sem("o_done"), sem("o_hi"), sem("o_free")
        conv = sem("conv_step")
        yc_done = sem("yc_done")
        wo_evac, wo_even = sem("wo_evac"), sem("wo_even")
        ple_gate = sem("ple_gate")
        ple_t, ple_s, ple_m, p_hi, p_lo = (sem(s) for s in ("ple_t", "ple_s", "ple_m", "p_hi", "p_lo"))

        NORM1 = 0
        xl_before = [KD * n for n in range(4)]
        X_AT = [None, 2, 2 + KD, 2 + 2 * KD]
        X_LAST = 2 + 3 * KD
        CONV_LAST, HEADS_FIRST, HEADS_LAST = 2 * CT - 2, CT - 1, 2 * CT - 1

        @block.sync
        def _(sp):
            def load(src, u, nk, i=0, stride=0, n=1):
                if PREVIOUS[u] is not None:
                    a, b = along(PREVIOUS, u, stride, n)
                    sp.wait_ge(lo_done, a + 1 + i * b)
                sp.dma_start(raw[:, SLOT[u], 0:nk * P], src).then_inc(raw_in[SLOT[u]], 16)

            sp.dma_start(par[:, :], params[:, :]).then_inc(par_in, 16)
            half = KD * P // 2
            sp.dma_start(raw[:, 0, 0:half], gu1[0, :, 0:half]).then_inc(first_in, 16)
            for c, (k, end) in enumerate(X_PIECES):
                sp.dma_start(x[:, k:end, :], xT[:, k:end, :]).then_inc(x_in[c], 16)
                if c == 2:
                    sp.dma_start(raw[:, 0, half:2 * half], gu1[0, :, half:2 * half]).then_inc(raw_in[0], 16)
            load(gu1[1], F1 + 1, KD)

            def ffn_loads(ff, gu, dn, done):
                for u in range(done, RAW):
                    load(gu[u], ff["u0"] + u, KD)
                n = N_GU // RAW - 1
                with sp.Fori(0, n) as i:
                    for j in range(RAW):
                        load(gu[bass.ds(i * RAW + RAW + j, 1)].rearrange("a p n -> (a p) n"),
                             ff["u0"] + RAW + j, KD, i, RAW, n)
                n = N_DN // RAW
                with sp.Fori(0, n) as i:
                    for j in range(RAW):
                        load(dn[bass.ds(i * RAW + j, 1)].rearrange("a p n -> (a p) n"),
                             ff["d0"] + j, KH, i, RAW, n)

            ffn_loads(FFN[0], gu1, dn1, 2)
            for u in range(3):
                load(w_in[u], MX + u, KD)
            with sp.Fori(0, CT - 1) as i:
                for j in range(6):
                    load(w_in[bass.ds(i * 6 + 3 + j, 1)].rearrange("a p n -> (a p) n"),
                         MX + 3 + j, KD, i, 6, CT - 1)
            for u in range(N_IN - 3, N_IN):
                load(w_in[u], MX + u, KD)
            for u in range(N_WO):
                load(w_out[u], WO + u, KD)
            ffn_loads(FFN[1], gu2, dn2, 0)
            sp.wait_ge(FFN[1]["hid"], KF)
            sp.dma_start(praw[:, :, :], pT[:, :, :]).then_inc(p_in, 16)
            for u in range(KD):
                load(ple[u], PL + u, KD + PK)
            for m in range(KD):
                sp.wait_ge(out_ready, m + 1)
                sp.dma_start(outT[:, m, :], x[:, m, :]).then_inc(stored, 16)
            sp.wait_ge(stored, 16 * KD)

        @block.gpsimd
        def _(pool):
            def select(t, op, base, pattern, mult, fill, step):
                pool.wait_ge(const_step, step)
                pool.affine_select(out=t, in_=t, compare_op=op, fill=fill, base=base, pattern=pattern,
                                   channel_multiplier=mult).then_inc(const_step, 1)

            pool.memset(one_col[:, :], 1.0).then_inc(const_step, 1)
            pool.memset(ones_f[:, :], 1.0).then_inc(const_step, 1)
            pool.memset(eps_col[:, :], EPS).then_inc(const_step, 1)

            def lo(u, nk, i=0, stride=0):
                pool.wait_ge(hi_done, u + 1 + i * stride)
                pool.tensor_tensor(wl[:, u % 2, 0:nk * P], raw[:, SLOT[u], 0:nk * P],
                                   wh[:, u % 2, 0:nk * P].bitcast(F32), ALU.subtract).then_inc(lo_done, 1)

            pool.wait_ge(const_step, 3)
            pool.tensor_copy(ones[:, :], ones_f[:, :]).then_inc(const_step, 1)

            half = KD * P // 2
            pool.wait_ge(first_hi, 1)
            pool.tensor_tensor(wl[:, 0, 0:half], raw[:, 0, 0:half], wh[:, 0, 0:half].bitcast(F32),
                               ALU.subtract).then_inc(first_lo, 1)
            pool.wait_ge(hi_done, 1)
            pool.tensor_tensor(wl[:, 0, half:2 * half], raw[:, 0, half:2 * half],
                               wh[:, 0, half:2 * half].bitcast(F32), ALU.subtract).then_inc(lo_done, 1)
            for k in range(POOL_SQ):
                pool.wait_ge(x_in[x_piece(k)], 16)
                pool.tensor_tensor(pool_sq[k][:, :], x[:, k, :], x[:, k, :], ALU.mult).then_inc(pool_sq_done, 1)
            lo(F1 + 1, KD)
            lo(F1 + 2, KD)
            fills = [(headones_f, 1.0), (tri_f, -1.0), (minus_f, -1.0), (ident, 0.0), (identb, 0.0), (blocked, 0.0)]
            for t, v in fills:
                pool.memset(t[:], v).then_inc(const_step, 1)
            n = 4 + len(fills)
            select(headones_f[:, 0:HD], ALU.is_ge, HD - 1, [[0, HD]], -1, 0.0, n)
            select(headones_f[:, HD:P], ALU.is_ge, -HD, [[0, HD]], 1, 0.0, n)
            select(tri_f[:, :], ALU.is_ge, 0, [[-1, P]], 1, 0.0, n)
            select(ident[:, :], ALU.not_equal, 0, [[-1, P]], 1, 1.0, n)
            select(identb[:, :], ALU.not_equal, 0, [[-1, P]], 1, 1.0, n)
            select(blocked[:, :, :], ALU.is_gt, 0, [[0, 2], [1, P]], -1, BLOCKED, n)

            pool.wait_ge(const_step, n + 6)
            pool.tensor_copy(negtri[:, :], tri_f[:, :]).then_inc(const_step, 1)
            pool.tensor_copy(negones[:, :], minus_f[:, :]).then_inc(const_step, 1)
            pool.tensor_copy(headones[:, :], headones_f[:, :]).then_inc(const_step, 1)

            def ffn(ff, first):
                u0, d0 = ff["u0"], ff["d0"]
                for u in range(first, RAW):
                    lo(u0 + u, KD)
                with pool.Fori(0, N_GU // RAW - 1) as i:
                    for j in range(RAW):
                        lo(u0 + RAW + j, KD, i, RAW)
                with pool.Fori(0, N_DN // RAW) as i:
                    for j in range(RAW):
                        lo(d0 + j, KH, i, RAW)

            ffn(FFN[0], 3)
            for u in range(MX, MX + 3):
                lo(u, KD)
            with pool.Fori(0, CT - 1) as i:
                for j in range(6):
                    lo(MX + 3 + j, KD, i, 6)
            for u in range(MX + N_IN - 3, F2):
                lo(u, KD)
            ffn(FFN[1], 0)
            for u in range(PL, UNITS):
                lo(u, KD + PK)

        @block.scalar
        def _(act):
            def hi(u, nk, i=0, stride=0, n=1):
                a, b = along(FILLS, u, stride, n)
                act.wait_ge(raw_in[SLOT[u]], 16 * a + i * (16 * b))
                if u >= 2:
                    act.wait_ge(unit_done, u - 1 + i * stride)
                act.activation(wh[:, u % 2, 0:nk * P], raw[:, SLOT[u], 0:nk * P], ACT.Copy).then_inc(hi_done, 1)

            def guess(norm):
                act.preload_act_table_set("natural_log_exp_and_others")
                act.wait_ge(var_done, norm + 1)
                act.activation(y0[:, :], var[:, :], ACT.Ln).then_inc(ln_done, 1)
                act.wait_ge(ln_done, norm + 1)
                act.activation(y0[:, :], y0[:, :], ACT.Exp, scale=-0.5).then_inc(guess_done, 1)

            half = KD * P // 2
            act.wait_ge(first_in, 16)
            act.activation(wh[:, 0, 0:half], raw[:, 0, 0:half], ACT.Copy).then_inc(first_hi, 1)
            act.wait_ge(par_in, 16)
            for k in range(KD):
                act.wait_ge(x_in[x_piece(k)], 16)
                act.activation(xh[:, k, :], x[:, k, :], ACT.Identity, scale=g_col(NORM1, k)).then_inc(xh_done, 1)
                if k == 3:
                    act.wait_ge(raw_in[0], 16)
                    act.activation(wh[:, 0, half:2 * half], raw[:, 0, half:2 * half], ACT.Copy).then_inc(hi_done, 1)
            hi(F1 + 1, KD)
            for k in range(POOL_SQ, KD):
                if k >= POOL_SQ + 2:
                    act.wait_ge(acc_done, k)
                act.activation(sq[:, k % 2, :], x[:, k, :], ACT.Square).then_inc(sq_done, 1)
                if k == 5:
                    hi(F1 + 2, KD)

            def new_x(norm, m, b, i=0, step=0):
                act.wait_ge(x_new, X_AT[norm] + m + 1 + i * step)
                act.wait_ge(acc_done, 9 * norm + m + i * step)
                if step:
                    act.nop(nofuse=True)
                    xm = x[:, bass.ds(i * step + m, 1), :]
                    dst = xh[:, bass.ds(i * step + m, 1), :]
                    gain = par[:, bass.ds(i * step + m + 8 * norm, 1)]
                else:
                    xm, dst, gain = x[:, m, :], xh[:, m, :], g_col(norm, m)
                act.activation(dst, xm, ACT.Identity, scale=gain).then_inc(xh_done, 1)
                act.activation(sq[:, b, :], xm, ACT.Square).then_inc(sq_done, 1)

            def ffn(ff, nxt, nxt_nk, norm):
                u0, d0 = ff["u0"], ff["d0"]

                def silu(f, b, i=0, step=0):
                    act.wait_ge(ff["banks"], 4 + 2 * f + 1 + i * 2 * step)
                    act.activation(act_in[:, b, :], act_in[:, b, :], ACT.Silu).then_inc(ff["silu"], 1)

                if norm > 1:
                    hi(u0 + 2, KD)
                guess(norm - 1)
                hi(u0 + 3, KD)
                silu(0, 0)
                hi(u0 + 4, KD)
                silu(1, 1)
                hi(u0 + 5, KD)
                n = N_GU // RAW - 2
                with act.Fori(0, n) as i:
                    hi(u0 + 6, KD, i, 4, n)
                    silu(2, 0, i, 2)
                    hi(u0 + 7, KD, i, 4, n)
                    hi(u0 + 8, KD, i, 4, n)
                    silu(3, 1, i, 2)
                    hi(u0 + 9, KD, i, 4, n)
                hi(u0 + N_GU - 2, KD)
                silu(KF - 2, 0)
                hi(u0 + N_GU - 1, KD)
                hi(d0, KH)
                silu(KF - 1, 1)
                hi(d0 + 1, KH)
                n = KD // 2 - 1
                with act.Fori(0, n) as i:
                    for j in range(2):
                        hi(d0 + 2 + 2 * j, KH, i, 4, n)
                        hi(d0 + 3 + 2 * j, KH, i, 4, n)
                        new_x(norm, j, j, i, 2)
                for m in range(KD - 2, KD):
                    for e in range(2):
                        u = d0 + 2 * m + 2 + e
                        if u < d0 + N_DN:
                            hi(u, KH)
                        else:
                            hi(nxt + u - d0 - N_DN, nxt_nk)
                    new_x(norm, m, m % 2)

            ffn(FFN[0], MX, KD, 1)

            def head_guess(c, i=0):
                act.wait_ge(hsum, c + 1 + i)
                if c or not isinstance(i, int):
                    act.wait_ge(qk_normed, c + i)
                act.activation(yq[:, :], ps[:, BN, :], ACT.Ln, scale=1.0 / HD, bias=eps_col[:, :]).then_inc(hln, 1)
                act.wait_ge(hln, c + 1 + i)
                act.activation(yq[:, :], yq[:, :], ACT.Exp, scale=-0.5).then_inc(hguess, 1)

            def softplus(j, n, z, i=0):
                act.wait_ge(z_ready, n + 1 + i)
                act.activation(att[j][:, :, :], z_of(j, z), ACT.Abs).then_inc(abs_done, 1)
                act.wait_ge(abs_done, n + 1 + i)
                act.activation(att[j][:, :, :], att[j][:, :, :], ACT.Exp, scale=-1.0).then_inc(e_done, 1)
                act.wait_ge(e_done, n + 1 + i)
                act.activation(att[j][:, :, :], att[j][:, :, :], ACT.Ln, bias=one_col[:, :]).then_inc(l_done, 1)

            def weights(j, n, z, i=0):
                act.wait_ge(later_done, n + 1 + i)
                act.activation(weight[j][:, :, :], z_of(j, z), ACT.Exp).then_inc(a_done, 1)

            def head_square(t, evac, i=0, count=None):
                act.wait_ge(m_evac, evac + i * 6)
                if count is not None:
                    act.wait_ge(hsum, count + i * 2)
                act.activation(sqh[:, :], t[:, :], ACT.Square).then_inc(head_sq_hi, 1)
                act.activation(sq[:, 0, :], t[:, :], ACT.Square).then_inc(head_sq, 1)

            def v_copy(c, i=0):
                act.wait_ge(v_turned, c + 1 + i)
                v = ps[:, BN, :].rearrange("p (b d) -> p b d", b=QB)
                act.activation(vtok[:, :, :], v, ACT.Copy).then_inc(v_ready, 1)

            def out_hi(c, i=None):
                act.wait_ge(o_done, (c if i is None else i) + 1)
                if i is None:
                    dst, src = yh[:, HEADS_LAST, :], ps[:, BO, :]
                else:
                    act.nop(nofuse=True)
                    dst, src = yh[:, bass.ds(i + HEADS_FIRST, 1), :], ps[:, BO:BO + 1, :]
                act.activation(dst, src, ACT.Copy).then_inc(o_hi, 1)

            hi(MX + 2, KD)
            guess(1)
            head_square(qt, 1)
            hi(MX + 3, KD)
            head_guess(0)
            head_square(kt, 2, count=1)
            hi(MX + 4, KD)

            def pair(i, last):
                c, one = (CT - 1, 0) if last else (0, i)
                i4, i2 = one * 4, one * 2
                b4, b2 = 4 * c, 2 * c
                B = MX + 3 + 6 * c
                n = CT - 1

                def hi6(local):
                    if last:
                        hi(B + local, KD)
                    else:
                        hi(B + local, KD, i, 6, n)
                head_guess(b2 + 1, i2)
                hi6(2)
                v_copy(c, one)
                softplus(3, b4, ZA, i4)
                softplus(2, b4 + 1, ZB, i4)
                hi6(3)
                hi6(4)
                act.wait_ge(tail_sum, b2 + 1 + i2)
                weights(3, b4, ZA, i4)
                weights(2, b4 + 1, ZB, i4)
                softplus(1, b4 + 2, ZA, i4)
                hi6(5)
                if not last:
                    head_square(qt, 7, i, 2)
                softplus(0, b4 + 3, ZB, i4)
                if not last:
                    head_guess(2, i2)
                    head_square(kt, 8, i, 3)
                hi6(6)
                if last:
                    hi6(7)
                act.wait_ge(tail_lo, b2 + 2 + i2)
                weights(1, b4 + 2, ZA, i4)
                weights(0, b4 + 3, ZB, i4)
                if not last:
                    hi6(7)
                    out_hi(0, i)
                else:
                    out_hi(CT - 1)

            with act.Fori(0, CT - 1) as i:
                pair(i, False)
            pair(0, True)
            hi(WO + 5, KD)
            for n in range(4):
                new_x(2, 2 * n, 0)
                hi(WO + 6 + n, KD)
                new_x(2, 2 * n + 1, 1)
            ffn(FFN[1], PL, KD + PK, 3)

            for k in range(PK):
                act.wait_ge(p_in, 16)
                act.activation(ph[:, k, :], praw[:, k, :], ACT.Copy).then_inc(p_hi, 1)
            hi(PL + 2, KD + PK)
            guess(3)
            for m in range(KD):
                if 3 <= m + 2 < KD:
                    hi(PL + m + 2, KD + PK)
                act.wait_ge(ple_t, m + 1)
                act.activation(act_in[:, m % 2, :], act_in[:, m % 2, :], ACT.Sigmoid).then_inc(ple_s, 1)

        @block.vector
        def _(dve):
            def rms_factor(norm):
                dve.wait_ge(sum_done, norm + 1)
                dve.tensor_scalar(var[:, :], ps[:, BN, :], 1.0 / D, EPS, ALU.mult, ALU.add).then_inc(var_done, 1)
                dve.wait_ge(guess_done, norm + 1)
                dve.scalar_tensor_tensor(nw[:, :], y0[:, :], -0.5, y0[:, :], ALU.mult, ALU.mult).then_inc(newton, 1)
                dve.wait_ge(newton, 2 * norm + 1)
                dve.tensor_tensor(nw[:, :], nw[:, :], var[:, :], ALU.mult).then_inc(newton, 1)
                dve.wait_ge(newton, 2 * norm + 2)
                dve.scalar_tensor_tensor(rms[:, :], nw[:, :], 1.5, y0[:, :], ALU.add, ALU.mult).then_inc(rms_done, 1)
                dve.wait_ge(rms_done, norm + 1)

            dve.memset(pad[:, 0:1], 0.0).then_inc(x_new, 2)
            dve.memset(pad[:, 1:2], 0.0).then_inc(FFN[0]["banks"], 4)
            dve.memset(pad[:, 2:3], 0.0).then_inc(FFN[1]["banks"], 4)
            dve.memset(pad[:, 3:4], 0.0).then_inc(o_free, 1)
            dve.wait_ge(par_in, 16)
            dve.tensor_scalar(gq8[:, :], gq, HD ** -0.5, None, ALU.mult).then_inc(gq_ok, 1)
            def new_sum(norm):
                dve.memset(sqacc[:, :], 0.0).then_inc(acc_done, 1)

            def add_square(norm, m, b, i=0, step=0):
                dve.wait_ge(sq_done, 8 * norm + m + 1 - POOL_SQ + i * step)
                dve.wait_ge(acc_done, 9 * norm + m + 1 + i * step)
                dve.tensor_tensor(sqacc[:, :], sqacc[:, :], sq[:, b, :], ALU.add).then_inc(acc_done, 1)

            def split_sum(norm):
                dve.wait_ge(acc_done, 9 * (norm + 1))
                dve.tensor_scalar(sqh[:, :], sqacc[:, :], 1.0, None, ALU.mult).then_inc(sum_hi, 1)
                dve.wait_ge(sum_hi, norm + 1)
                dve.tensor_tensor(sql[:, :], sqacc[:, :], sqh[:, :].bitcast(F32), ALU.subtract).then_inc(sum_lo, 1)

            new_sum(0)
            for k in range(KD):
                dve.wait_ge(xh_done, k + 1)
                dve.scalar_tensor_tensor(xl[:, k, :], x[:, k, :], g_col(NORM1, k), xh[:, k, :].bitcast(F32),
                                         ALU.mult, ALU.subtract).then_inc(xl_done, 1)
            for k in range(POOL_SQ):
                dve.wait_ge(pool_sq_done, k + 1)
                dve.wait_ge(acc_done, k + 1)
                dve.tensor_tensor(sqacc[:, :], sqacc[:, :], pool_sq[k][:, :], ALU.add).then_inc(acc_done, 1)
            for k in range(POOL_SQ, KD):
                add_square(0, k, k % 2)
            split_sum(0)

            def new_x(norm, m, bank, scale, i=0, step=0, add=True):
                if step:
                    at = bass.ds(i * step + m, 1)
                    xm, h, l = x[:, at, :], xh[:, at, :], xl[:, at, :]
                    gain = par[:, bass.ds(i * step + m + 8 * norm, 1)]
                    src = ps[:, bank:bank + 1, :]
                else:
                    xm, h, l, gain, src = x[:, m, :], xh[:, m, :], xl[:, m, :], g_col(norm, m), ps[:, bank, :]
                dve.scalar_tensor_tensor(xm, src, scale, xm, ALU.mult, ALU.add).then_inc(x_new, 1)
                dve.wait_ge(xh_done, 8 * norm + m + 1 + i * step)
                dve.scalar_tensor_tensor(l, xm, gain, h.bitcast(F32), ALU.mult, ALU.subtract).then_inc(xl_done, 1)
                if add:
                    add_square(norm, m, m % 2, i, step)

            def ffn(ff, norm):
                u0, d0 = ff["u0"], ff["d0"]
                rms_factor(norm - 1)
                n = KF // 2
                with dve.Fori(0, n) as i:
                    for b in range(2):
                        dve.wait_ge(unit_done, u0 + 2 * b + 1 + i * 4)
                        dve.tensor_tensor(act_in[:, b, :], ps[:, 2 * b, :], rms[:, :], ALU.mult).then_inc(ff["banks"], 1)
                        dve.wait_ge(unit_done, u0 + 2 * b + 2 + i * 4)
                        dve.tensor_tensor(upr[:, :], ps[:, 2 * b + 1, :], rms[:, :], ALU.mult).then_inc(ff["banks"], 1)
                        dve.wait_ge(ff["banks"], 4 + 2 * b + 2 + i * 4)
                        dve.wait_ge(ff["silu"], b + 1 + i * 2)
                        dve.tensor_tensor(hid[:, :], act_in[:, b, :], upr[:, :], ALU.mult).then_inc(ff["hid"], 1)
                        dve.wait_ge(ff["hid"], b + 1 + i * 2)
                        at = bass.ds(i * 2 + b, 1)
                        dve.tensor_scalar(hh[:, at, :], hid[:, :], 1.0, None, ALU.mult).then_inc(ff["hh"], 1)
                        dve.wait_ge(ff["hh"], b + 1 + i * 2)
                        dve.tensor_tensor(hl[:, at, :], hid[:, :], hh[:, at, :].bitcast(F32),
                                          ALU.subtract).then_inc(ff["hl"], 1)
                new_sum(norm)
                with dve.Fori(0, KD // 2) as i:
                    for j in range(2):
                        dve.wait_ge(unit_done, d0 + 2 * j + 2 + i * 4)
                        new_x(norm, j, j, 0.5, i, 2)

            ffn(FFN[0], 1)
            split_sum(1)

            def evac(dst, unit, bank, i=0):
                dve.wait_ge(unit_done, unit + 1 + i * 6)
                dve.tensor_tensor(dst[:, :], ps[:, bank, :], rms[:, :], ALU.mult).then_inc(m_evac, 1)

            def square_lo(c, i=0):
                dve.wait_ge(head_sq_hi, c + 1 + i)
                dve.wait_ge(head_sq, c + 1 + i)
                dve.tensor_tensor(sql[:, :], sq[:, 0, :], sqh[:, :].bitcast(F32), ALU.subtract).then_inc(head_sq_lo, 1)

            def head_norm(c, t, gain, i=0):
                is_q = t is qt
                dve.wait_ge(hguess, c + 1 + i)
                dve.scalar_tensor_tensor(t[:, :], t[:, :], gain, yq[:, :], ALU.mult, ALU.mult).then_inc(qk_normed, 1)
                dve.wait_ge(qk_normed, c + 1 + i)
                for h in range(2):
                    dst = qhh[h] if is_q else khl[h]
                    dve.tensor_scalar(dst[OWN[h], :], t[OWN[h], :], 1.0, None, ALU.mult).then_inc(qk_hi, 1)
                for h in range(2):
                    hi = qhh[h] if is_q else khl[h]
                    lo = qll[h][OWN[h], :] if is_q else khl[h][OWN[1 - h], :]
                    dve.wait_ge(qk_hi, 2 * c + 1 + h + i * 2)
                    dve.tensor_tensor(lo, t[OWN[h], :], hi[OWN[h], :].bitcast(F32), ALU.subtract).then_inc(qk_lo, 1)
                if is_q:
                    for h in range(2):
                        dve.tensor_scalar(qhh[h][OWN[1 - h], :], t[OWN[h], :], 1.0, None, ALU.mult).then_inc(q_twice, 1)
                        dve.tensor_tensor(qll[h][OWN[1 - h], :], t[OWN[h], :], qhh[h][OWN[h], :].bitcast(F32),
                                          ALU.subtract).then_inc(q_twice, 1)

            def softplus(j, n, z, i=0):
                dve.wait_ge(l_done, n + 1 + i)
                dve.scalar_tensor_tensor(att[j][:, :, :], z_of(j, z), 0.0, att[j][:, :, :],
                                         ALU.max, ALU.add).then_inc(sp_done, 1)
                dve.wait_ge(sp_done, n + 1 + i)
                dve.tensor_scalar(sph[j][:, :, :], att[j][:, :, :], 1.0, None, ALU.mult).then_inc(sp_hi, 1)
                dve.wait_ge(sp_hi, n + 1 + i)
                dve.tensor_tensor(spl[j][:, :, :], att[j][:, :, :], sph[j][:, :, :].bitcast(F32),
                                  ALU.subtract).then_inc(sp_lo, 1)

            def add_tail(j, n, i=0):
                dve.wait_ge(sp_lo, 2 * n + (2 if j == 2 else 1) + i * 2)
                dve.tensor_tensor(att[j][:, :, P:T - P * j], att[j][:, :, P:T - P * j], att[j + 1][:, :, :],
                                  ALU.add).then_inc(tail_sum, 1)

            def split_tail(j, n, i=0):
                dve.wait_ge(tail_sum, n + 1 + i)
                dve.tensor_scalar(tail_h[j][:, :, :], att[j][:, :, :], 1.0, None, ALU.mult).then_inc(tail_hi, 1)
                dve.wait_ge(tail_hi, n + 1 + i)
                dve.tensor_tensor(tail_l[j][:, :, :], att[j][:, :, :], tail_h[j][:, :, :].bitcast(F32),
                                  ALU.subtract).then_inc(tail_lo, 1)

            rms_factor(1)
            evac(qt, MX, 0)
            square_lo(0)
            evac(kt, MX + 1, 1)
            evac(vt, MX + 2, BO)
            square_lo(1)
            dve.wait_ge(gq_ok, 1)
            head_norm(0, qt, gq8[:, :])

            def pair(i, last):
                c, one = (CT - 1, 0) if last else (0, i)
                i2, i4 = one * 2, one * 4
                B = MX + 3 + 6 * c
                n_conv = 5 * c
                i5 = one * 5

                def bank(local):
                    return (3 + local) % 2

                def ev(dst, local):
                    evac(dst, B + local, bank(local), one)
                head_norm(2 * c + 1, kt, gk, i2)
                ev(bt, 0)
                ev(cgate, 1)
                softplus(3, 4 * c, ZA, i4)
                softplus(2, 4 * c + 1, ZB, i4)
                add_tail(2, 2 * c, i2)
                ev(ut, 2)
                dve.wait_ge(m_evac, 6 * c + 6 + one * 6)
                dve.tensor_tensor(cgate[:, :], cgate[:, :], ut[:, :], ALU.mult).then_inc(conv, 1)
                dve.wait_ge(conv, n_conv + 1 + i5)
                if last:
                    w = [conv_w(c, tap) for tap in range(3)]
                    bias = conv_b(c)
                    y_hi, y_lo = yh[:, CONV_LAST, :], yl[:, CONV_LAST, :]
                else:
                    w = [par[:, bass.ds(i * 3 + (32 + tap), 1)] for tap in range(3)]
                    bias = par[:, bass.ds(i + 44, 1)]
                    y_hi, y_lo = yh[:, bass.ds(i, 1), :], yl[:, bass.ds(i, 1), :]
                dve.tensor_scalar(ut[:, :], cgate[:, :], w[2], bias, ALU.mult, ALU.add).then_inc(conv, 1)
                dve.wait_ge(conv, n_conv + 2 + i5)
                dve.scalar_tensor_tensor(ut[:, 1:T], cgate[:, 0:T - 1], w[1], ut[:, 1:T],
                                         ALU.mult, ALU.add).then_inc(conv, 1)
                dve.wait_ge(conv, n_conv + 3 + i5)
                dve.scalar_tensor_tensor(ut[:, 2:T], cgate[:, 0:T - 2], w[0], ut[:, 2:T],
                                         ALU.mult, ALU.add).then_inc(conv, 1)
                dve.wait_ge(conv, n_conv + 4 + i5)
                dve.tensor_tensor(ut[:, :], ut[:, :], bt[:, :], ALU.mult).then_inc(conv, 1)
                dve.wait_ge(conv, n_conv + 5 + i5)
                dve.tensor_scalar(y_hi, ut[:, :], 1.0, None, ALU.mult).then_inc(yc_done, 1)
                dve.wait_ge(yc_done, 2 * c + 1 + i2)
                dve.tensor_tensor(y_lo, ut[:, :], y_hi.bitcast(F32), ALU.subtract).then_inc(yc_done, 1)
                dve.wait_ge(later_done, 4 * c + 2 + i4)
                split_tail(2, 2 * c, i2)
                if last:
                    for m in range(3):
                        add_out(m, m % 2)
                else:
                    ev(qt, 3)
                softplus(1, 4 * c + 2, ZA, i4)
                if last:
                    add_out(3, 1)
                else:
                    square_lo(2, i2)
                add_tail(1, 2 * c + 1, i2)
                split_tail(1, 2 * c + 1, i2)
                softplus(0, 4 * c + 3, ZB, i4)
                if not last:
                    ev(kt, 4)
                    head_norm(2, qt, gq8[:, :], i2)
                    square_lo(3, i2)
                    dve.wait_ge(v_turned, 1 + i)
                    ev(vt, 5)
                    at = bass.ds(i + HEADS_FIRST, 1)
                    dve.wait_ge(o_hi, i + 1)
                    dve.tensor_tensor(yl[:, at, :], ps[:, BO:BO + 1, :], yh[:, at, :].bitcast(F32),
                                      ALU.subtract).then_inc(o_free, 1)
                else:
                    for m in range(4, KD - 1):
                        add_out(m, m % 2)
                    dve.wait_ge(o_hi, CT)
                    dve.tensor_tensor(yl[:, HEADS_LAST, :], ps[:, BO, :], yh[:, HEADS_LAST, :].bitcast(F32),
                                      ALU.subtract).then_inc(o_free, 1)
                    add_out(KD - 1, 1)

            def wo_tile_done(half):
                if half % 2:
                    dve.wait_ge(unit_done, WO + half // 2 + 1)
                else:
                    dve.wait_ge(wo_even, half // 2 + 1)

            def add_out(m, bank):
                wo_tile_done(m)
                dve.tensor_tensor(x[:, m, :], ps[:, bank, :], x[:, m, :], ALU.add).then_inc(wo_evac, 1)

            with dve.Fori(0, CT - 1) as i:
                pair(i, False)
            pair(0, True)
            dve.wait_ge(wo_evac, KD)
            new_sum(2)
            for m in range(KD):
                wo_tile_done(KD + m)
                new_x(2, m, m % 2, 1.0, add=False)
                if m:
                    add_square(2, m - 1, (m - 1) % 2)
            add_square(2, KD - 1, 1)
            split_sum(2)
            ffn(FFN[1], 3)

            for k in range(PK):
                dve.wait_ge(p_hi, k + 1)
                dve.tensor_tensor(pl[:, k, :], praw[:, k, :], ph[:, k, :].bitcast(F32), ALU.subtract).then_inc(p_lo, 1)
            split_sum(3)
            rms_factor(3)
            for m in range(KD):
                b, bank = m % 2, 2 * (m % 3)
                dve.wait_ge(ple_gate, m + 1)
                dve.tensor_tensor(act_in[:, b, :], ps[:, bank, :], rms[:, :], ALU.mult).then_inc(ple_t, 1)
                dve.wait_ge(unit_done, PL + m + 1)
                dve.wait_ge(ple_s, m + 1)
                dve.tensor_tensor(upr[:, :], ps[:, bank + 1, :], act_in[:, b, :], ALU.mult).then_inc(ple_m, 1)
                dve.wait_ge(ple_m, m + 1)
                dve.tensor_tensor(x[:, m, :], x[:, m, :], upr[:, :], ALU.add).then_inc(out_ready, 1)

        @block.tensor
        def _(pe):
            def products(u, bank, ks, at, mh, ml, ready=None, first=True, last=True, i=0, stride=0, inc=unit_done):
                b = u % 2
                w_hi = [wh[:, b, a * P:(a + 1) * P] for a in at]
                w_lo = [wl[:, b, a * P:(a + 1) * P] for a in at]
                pe.wait_ge(*((first_hi, 1) if u == 0 and isinstance(i, int) else (hi_done, u + 1 + i * stride)))
                for n, k in enumerate(ks):
                    if u == 0 and isinstance(i, int) and n == KD // 2:
                        pe.wait_ge(hi_done, 1)
                    if ready is not None:
                        pe.wait_ge(ready[0], ready[1] + k + 1)
                    pe.matmul(ps[:, bank, :], w_hi[n], mh[:, k, :], start=first and n == 0, stop=False)
                    pe.matmul(ps[:, bank, :], w_hi[n], ml[:, k, :], start=False, stop=False)
                pe.wait_ge(lo_done, u + 1 + i * stride)
                for n, k in enumerate(ks):
                    mm = pe.matmul(ps[:, bank, :], w_lo[n], mh[:, k, :], start=False, stop=last and n == len(ks) - 1)
                if inc is not None:
                    mm.then_inc(inc, 1)

            def sum_squares(norm):
                if norm:
                    pe.wait_ge(var_done, norm)
                pe.wait_ge(sum_lo, norm + 1)
                pe.matmul(ps[:, BN, :], ones[:, :], sqh[:, :], start=True, stop=False)
                pe.matmul(ps[:, BN, :], ones[:, :], sql[:, :], start=False, stop=True).then_inc(sum_done, 1)

            K8 = range(KD)

            def with_sum(u, bank, norm, k):
                products(u, bank, range(k), range(k), xh, xl, last=False, inc=None)
                sum_squares(norm)
                products(u, bank, range(k, KD), range(k, KD), xh, xl, first=False)

            def ffn(ff, norm):
                u0, d0 = ff["u0"], ff["d0"]
                ready = (xl_done, xl_before[norm])

                def four(i, base, peeled):
                    for j in range(4):
                        pe.wait_ge(ff["banks"], base + j + 1 + i * 4)
                        if peeled and norm and j < 2:
                            pe.wait_ge(x_new, X_AT[norm + 1] - 1 + j)
                        if peeled and j == (1 if norm else 2):
                            with_sum(u0 + j, j, norm, KD - 1 if norm else 1)
                        else:
                            products(u0 + base + j, j, K8, K8, xh, xl, ready if j == 0 and peeled else None, i=i, stride=4)
                four(0, 0, True)
                with pe.Fori(0, N_GU // 4 - 1) as i:
                    four(i, 4, False)
                pe.wait_ge(ff["banks"], 4 + N_GU - 2)
                with pe.Fori(0, KD // 2) as i:
                    for j in range(2):
                        pe.wait_ge(x_new, X_AT[norm + 1] - 1 + j + i * 2)
                        for e in range(2):
                            pe.wait_ge(ff["hl"], KH * (e + 1))
                            products(d0 + 2 * j + e, j, range(e * KH, (e + 1) * KH), range(KH), hh, hl,
                                     first=e == 0, last=e == 1, i=i, stride=4)

            pe.wait_ge(const_step, 4)
            ffn(FFN[0], 0)

            pe.wait_ge(const_step, 19)

            def proj(u, ks, evacs, i=0):
                if ks[0] == 0:
                    pe.wait_ge(m_evac, evacs + i * 6)
                products(u, (u - MX) % 2, ks, ks, xh, xl, first=ks[0] == 0, last=ks[-1] == KD - 1, i=i, stride=6,
                         inc=unit_done if ks[-1] == KD - 1 else None)

            def head_sum(c, i=0):
                pe.wait_ge(head_sq_lo, c + 1 + i)
                pe.matmul(ps[:, BN, :], headones[:, :], sqh[:, :], start=True, stop=False)
                pe.matmul(ps[:, BN, :], headones[:, :], sql[:, :], start=False, stop=True).then_inc(hsum, 1)

            def heads_of(j):
                return [slice(0, 2)] if 2 * (T - P * j) <= T else range(2)

            def scores(j, z):
                out = z_of(j, z)
                joint = 2 * (T - P * j) <= T
                for h in range(2):
                    for part in (qhh, qll):
                        pe.matmul(out[:, h, :], khl[h][:, P * j:P * j + P], part[h][:, P * j:T],
                                  start=part is qhh and (h == 0 or not joint), stop=False, skip_group_check=True)
                for h in heads_of(j):
                    mm = pe.matmul(out[:, h, 0:P], identb[:, :], blocked[:, h, :], start=False, stop=False,
                                   skip_group_check=True)
                mm.then_inc(z_ready, 1)

            def minus_later(j, n, z, i=0, tails=None):
                pe.wait_ge(sp_lo, n + 1 + i)
                out = z_of(j, z)
                if tails is not None:
                    pe.wait_ge(tail_lo, tails)
                sums = [(negtri, 0, sph[j], spl[j])]
                if j < QB - 1:
                    sums.append((negones, P, tail_h[j + 1], tail_l[j + 1]))
                for h in heads_of(j):
                    for minus, first, *parts in sums:
                        for part in parts:
                            mm = pe.matmul(out[:, h, first:T - P * j], minus[:, :], part[:, h, :], start=False,
                                           stop=minus is sums[-1][0] and part is parts[1], skip_group_check=True)
                mm.then_inc(later_done, 1)

            def values(j, n, i=0):
                pe.wait_ge(a_done, n + 1 + i)
                for h in range(2):
                    rows = slice(HD * h, HD * h + HD)
                    mm = pe.matmul(ps[rows, BO, P * j:T], vtok[:, j, rows], weight[j][:, h, :],
                                   start=j == QB - 1, stop=j == 0, skip_group_check=True)
                return mm

            ready = (xl_done, xl_before[1])
            pe.wait_ge(x_new, X_AT[2] - 1)
            products(MX, 0, K8, K8, xh, xl, ready, i=0)
            pe.wait_ge(x_new, X_AT[2])
            with_sum(MX + 1, 1, 1, 3)
            products(MX + 2, BO, range(6), range(6), xh, xl, last=False, inc=None)
            pe.wait_ge(var_done, 2)
            head_sum(0)
            products(MX + 2, BO, range(6, KD), range(6, KD), xh, xl, first=False)

            def pair(i, last):
                c, one = (CT - 1, 0) if last else (0, i)
                i2, i4 = one * 2, one * 4
                B = MX + 3 + 6 * c
                E = 3 + 6 * c

                def part(local, ks):
                    proj(B + local, ks, E + local - 1, one)
                A, Z, ALL = range(4), range(4, 8), range(8)
                part(0, A)
                pe.wait_ge(hln, 2 * c + 1 + i2)
                head_sum(2 * c + 1, i2)
                part(0, Z)
                pe.wait_ge(m_evac, E + one * 6)
                pe.wait_ge(hln, 2 * c + 2 + i2)
                for b in range(QB):
                    mm = pe.transpose(ps[:, BN, P * b:P * b + P], vt[:, P * b:P * b + P], ident[:, :])
                mm.then_inc(v_turned, 1)
                part(1, A)
                pe.wait_ge(qk_lo, 4 * c + 4 + i4)
                pe.wait_ge(q_twice, 4 * c + 4 + i4)
                scores(3, ZA)
                scores(2, ZB)
                part(1, Z)
                part(2, ALL)
                minus_later(3, 4 * c, ZA, i4)
                minus_later(2, 4 * c + 1, ZB, i4)
                if last:
                    wo_tile(0)
                    wo_tile(1)
                else:
                    part(3, A)
                pe.wait_ge(v_ready, c + 1 + one)
                pe.wait_ge(o_free, c + 1 + one)
                values(3, 4 * c, i4)
                values(2, 4 * c + 1, i4)
                scores(1, ZA)
                scores(0, ZB)
                if last:
                    for m in range(2, 6):
                        wo_tile(m)
                else:
                    part(3, Z)
                    part(4, A)
                    part(4, Z)
                    pe.wait_ge(v_ready, 1 + one)
                    head_sum(2, i2)
                    part(5, A)
                minus_later(1, 4 * c + 2, ZA, i4, 2 * c + 1 + i2)
                minus_later(0, 4 * c + 3, ZB, i4, 2 * c + 2 + i2)
                if last:
                    wo_tile(6)
                else:
                    part(5, Z)
                values(1, 4 * c + 2, i4)
                values(0, 4 * c + 3, i4).then_inc(o_done, 1)

            def wo_tile(half):
                m, later = half % KD, half // KD
                if half < 2:
                    pe.wait_ge(m_evac, N_IN - 1 + m)
                elif half < KD + 2:
                    pe.wait_ge(wo_evac, half - 1)
                else:
                    pe.wait_ge(x_new, X_AT[2] + m - 1)
                u, odd = WO + half // 2, m % 2
                pe.wait_ge(lo_done, u + 1)
                for k in range(4):
                    if not later and k == 0:
                        pe.wait_ge(yc_done, 2 * (CT - 1))
                        pe.wait_ge(o_free, 2)
                    if later and k == 2:
                        pe.wait_ge(yc_done, 2 * CT)
                    if later and k == 3:
                        pe.wait_ge(o_free, CT + 1)
                    a, y = 4 * odd + k, 4 * later + k
                    w_hi, w_lo = wh[:, u % 2, a * P:(a + 1) * P], wl[:, u % 2, a * P:(a + 1) * P]
                    pe.matmul(ps[:, odd, :], w_hi, yh[:, y, :], start=k == 0, stop=False)
                    pe.matmul(ps[:, odd, :], w_lo, yh[:, y, :], start=False, stop=False)
                    mm = pe.matmul(ps[:, odd, :], w_hi, yl[:, y, :], start=False, stop=k == 3)
                mm.then_inc(wo_even if not odd else unit_done, 1)

            with pe.Fori(0, CT - 1) as i:
                pair(i, False)
            pair(0, True)
            for half in range(KD - 1, 2 * KD):
                wo_tile(half)
            ffn(FFN[1], 2)

            for m in range(KD):
                b, u = m % 3, PL + m
                if m == 0:
                    pe.wait_ge(x_new, X_LAST - 1)
                elif m == 1:
                    pe.wait_ge(FFN[1]["banks"], 4 + N_GU)
                elif m > 2:
                    pe.wait_ge(ple_m, m - 2)
                products(u, 2 * b, K8, K8, xh, xl, (xl_done, xl_before[3]) if m == 0 else None, inc=ple_gate)
                if m == 0:
                    pe.wait_ge(x_new, X_LAST)
                    pe.wait_ge(p_lo, PK)
                products(u, 2 * b + 1, range(PK), range(KD, KD + PK), ph, pl)
                if m == 0:
                    sum_squares(3)


def kernel(**inputs):
    import concourse.bacc as bacc
    from concourse.bass_utils import run_bass_kernel_spmd

    a = {name: np.asarray(v) for name, v in inputs.items()}
    rows = np.ascontiguousarray

    def feature_major(t, tiles):
        return rows(t.T.reshape(tiles, P, T).transpose(1, 0, 2))

    def k_tiles(w, k):
        return w.reshape(k, P, w.shape[1] // P, P).transpose(2, 1, 0, 3)

    def gate_up(g, u):
        return rows(np.stack([k_tiles(g, KD), k_tiles(u, KD)], axis=1).reshape(N_GU, P, KD * P))

    def down(w):
        return rows(k_tiles(w, KF).reshape(KD, P, 2, KH * P).transpose(0, 2, 1, 3).reshape(N_DN, P, KH * P))

    groups = k_tiles(a["w_in"][0], KD).reshape(6, CT, P, KD * P)
    order = [(g, 0) for g in (3, 4, 5)]
    for t in range(CT):
        order += [(g, t) for g in (0, 1, 2)]
        if t + 1 < CT:
            order += [(g, t + 1) for g in (3, 4, 5)]
    w_in = np.stack([groups[g, t] for g, t in order])
    w_out = a["w_out"][0].reshape(KD, P, D)[[0, 1, 2, 4, 5, 6, 3, 7]]
    w_out = w_out.reshape(2, 4, P, 4, 2, P).transpose(0, 3, 2, 4, 1, 5)
    ple = np.concatenate([k_tiles(a["ple_w_gate"][0], KD), k_tiles(a["ple_w_proj"][0], PK)], axis=2)

    def columns(v, n):
        return v.reshape(n, P).T

    norms = [columns(a[n][0], KD) for n in ("ffn1_norm", "mix_norm", "ffn2_norm", "ple_norm")]
    conv_w = a["conv_w"][0].reshape(3, CT, P).transpose(2, 1, 0).reshape(P, 3 * CT)
    heads = [np.concatenate([a[n][0], a[n][0]]).reshape(P, 1) for n in ("q_norm", "k_norm")]
    params = np.concatenate(norms + [conv_w, columns(a["conv_b"][0], CT)] + heads, axis=1)

    arrays = {
        "xT": feature_major(a["x"][0], KD), "pT": feature_major(a["p"][0, 0], PK), "params": rows(params),
        "gu1": gate_up(a["ffn1_w_gate"][0], a["ffn1_w_up"][0]), "dn1": down(a["ffn1_w_down"][0]),
        "w_in": rows(w_in), "w_out": rows(w_out.reshape(N_WO, P, KD * P)),
        "gu2": gate_up(a["ffn2_w_gate"][0], a["ffn2_w_up"][0]), "dn2": down(a["ffn2_w_down"][0]),
        "ple": rows(ple.reshape(KD, P, (KD + PK) * P)),
    }
    nc = bacc.Bacc("TRN2", target_bir_lowering=False, num_devices=1)
    args = [nc.dram_tensor(name, v.shape, mybir.dt.from_np(v.dtype), kind="ExternalInput").ap()
            for name, v in arrays.items()]
    args.append(nc.dram_tensor("outT", (P, KD, T), F32, kind="ExternalOutput").ap())
    build(nc, *args)
    r = run_bass_kernel_spmd(nc, [arrays], core_ids=[0])
    out = r.results[0]["outT"]
    return rows(out.transpose(2, 1, 0).reshape(1, T, D))
```
